# Optimizing a Trainium2 kernel written in Bass

```python
import math
import jax, jax.numpy as jnp
from jax import lax
import numpy as np

D_MODEL = 2048
BATCH = 1
SEQ = 256
DEPTH = 2

CHUNK = 64
N_MIXERS = 2
HEAD_DIM = 64
N_HEADS = D_MODEL // HEAD_DIM
N_KV_HEADS = N_HEADS // 8
GROUP = N_HEADS // N_KV_HEADS
WINDOW = 128
WINDOW_CHUNKS = WINDOW // CHUNK
QKV_DIM = (N_HEADS + 2 * N_KV_HEADS) * HEAD_DIM
ROPE_THETA = 10000.0
LRU_WIDTH = D_MODEL
GATE_BLOCKS = 8
GATE_BLOCK_W = LRU_WIDTH // GATE_BLOCKS
CONV_WIDTH = 4
LRU_C = 8.0
D_FF = 4 * D_MODEL
NORM_EPS = 1e-6
NEG_INF = -1e30

kernel_name = "hybrid_swa_sink_rglru_sqrelu_trunk"

def rms_norm(x, g):
    xf = x.astype(jnp.float32)
    y = xf * lax.rsqrt(jnp.mean(xf * xf, axis=-1, keepdims=True) + NORM_EPS)
    return (y * g.astype(jnp.float32)).astype(x.dtype)

def rope(x, pos):
    half = x.shape[-1] // 2
    freqs = ROPE_THETA ** (-jnp.arange(half, dtype=jnp.float32) / half)
    ang = pos[:, None] * freqs[None, :]
    cos = jnp.cos(ang)[None, :, None, :]
    sin = jnp.sin(ang)[None, :, None, :]
    xf = x.astype(jnp.float32)
    x1, x2 = xf[..., :half], xf[..., half:]
    out = jnp.concatenate([x1 * cos - x2 * sin, x2 * cos + x1 * sin], axis=-1)
    return out.astype(x.dtype)

def swa_sink_attention(h, w_qkv, b_qkv, sinks, w_o, b_o):
    B, S, _ = h.shape
    nc = S // CHUNK
    qkv = h @ w_qkv + b_qkv
    q = qkv[..., : N_HEADS * HEAD_DIM].reshape(B, S, N_HEADS, HEAD_DIM)
    k = qkv[..., N_HEADS * HEAD_DIM: (N_HEADS + N_KV_HEADS) * HEAD_DIM].reshape(B, S, N_KV_HEADS, HEAD_DIM)
    v = qkv[..., (N_HEADS + N_KV_HEADS) * HEAD_DIM:].reshape(B, S, N_KV_HEADS, HEAD_DIM)
    pos = jnp.arange(S, dtype=jnp.float32)
    q = rope(q, pos)
    k = rope(k, pos)
    qb = q.reshape(B, nc, CHUNK, N_KV_HEADS, GROUP, HEAD_DIM)
    pad = ((0, 0), (WINDOW_CHUNKS - 1, 0), (0, 0), (0, 0), (0, 0))
    kp = jnp.pad(k.reshape(B, nc, CHUNK, N_KV_HEADS, HEAD_DIM), pad)
    vp = jnp.pad(v.reshape(B, nc, CHUNK, N_KV_HEADS, HEAD_DIM), pad)
    k_band = jnp.concatenate([kp[:, j:j + nc] for j in range(WINDOW_CHUNKS)], axis=2)
    v_band = jnp.concatenate([vp[:, j:j + nc] for j in range(WINDOW_CHUNKS)], axis=2)
    key_chunk = (jnp.arange(nc)[:, None] - (WINDOW_CHUNKS - 1)
                 + (jnp.arange(WINDOW_CHUNKS * CHUNK) // CHUNK)[None, :])
    valid = (key_chunk >= 0)[None, :, None, None, None, :]
    scale = 1.0 / math.sqrt(HEAD_DIM)
    scores = jnp.einsum('bcqkgd,bcskd->bckgqs', qb.astype(jnp.float32),
                        k_band.astype(jnp.float32)) * scale
    scores = jnp.where(valid, scores, NEG_INF)
    sink = sinks.astype(jnp.float32).reshape(N_KV_HEADS, GROUP)[None, None, :, :, None, None]
    sink = jnp.broadcast_to(sink, scores.shape[:-1] + (1,))
    probs = jax.nn.softmax(jnp.concatenate([scores, sink], axis=-1), axis=-1)[..., :-1]
    out = jnp.einsum('bckgqs,bcskd->bcqkgd', probs.astype(v.dtype), v_band)
    out = out.reshape(B, S, N_HEADS * HEAD_DIM)
    return out @ w_o + b_o

def rglru_block(h, w_in, b_in, conv_w, conv_b, gate_a_w, gate_a_b, gate_x_w, gate_x_b, lam, w_out, b_out):
    B, S, _ = h.shape
    proj = h @ w_in + b_in
    y_br = jax.nn.gelu(proj[..., :LRU_WIDTH], approximate=True)
    x_br = proj[..., LRU_WIDTH:]
    xp = jnp.pad(x_br, ((0, 0), (CONV_WIDTH - 1, 0), (0, 0)))
    xc = conv_b
    for tap in range(CONV_WIDTH):
        xc = xc + xp[:, tap:tap + S] * conv_w[tap]
    xh = xc.reshape(B, S, GATE_BLOCKS, GATE_BLOCK_W)
    r = jax.nn.sigmoid((jnp.einsum('bsnd,nde->bsne', xh, gate_a_w).reshape(B, S, LRU_WIDTH)
                        + gate_a_b).astype(jnp.float32))
    i = jax.nn.sigmoid((jnp.einsum('bsnd,nde->bsne', xh, gate_x_w).reshape(B, S, LRU_WIDTH)
                        + gate_x_b).astype(jnp.float32))
    log_a = -LRU_C * r * jax.nn.softplus(-lam.astype(jnp.float32))
    a = jnp.exp(log_a)
    mult = jnp.sqrt(-jnp.expm1(2.0 * log_a))
    u = mult * (i * xc.astype(jnp.float32))

    def step(carry, inp):
        a_t, u_t = inp
        carry = a_t * carry + u_t
        return carry, carry

    h0 = jnp.zeros((B, LRU_WIDTH), jnp.float32)
    _, hs = lax.scan(step, h0, (jnp.swapaxes(a, 0, 1), jnp.swapaxes(u, 0, 1)))
    hs = jnp.swapaxes(hs, 0, 1).astype(h.dtype)
    return (hs * y_br) @ w_out + b_out

def sqrelu_mlp(h, w_up, w_down):
    return jnp.square(jax.nn.relu(h @ w_up)) @ w_down

def setup_inputs(seed: int = 0) -> dict:
    key = jax.random.key(seed)
    ks = iter(jax.random.split(key, 32))
    n_a = (DEPTH + N_MIXERS - 1) // N_MIXERS
    n_b = DEPTH // N_MIXERS
    f32 = jnp.float32

    def nrm(shape, fan_in):
        return jax.random.normal(next(ks), shape, f32) * (fan_in ** -0.5)

    def small(shape, s=0.01):
        return jax.random.normal(next(ks), shape, f32) * s

    x = jax.random.normal(next(ks), (BATCH, SEQ, D_MODEL), f32)
    mix_norm = 1.0 + small((DEPTH, D_MODEL), 0.05)
    mlp_norm = 1.0 + small((DEPTH, D_MODEL), 0.05)
    final_norm = 1.0 + small((D_MODEL,), 0.05)
    a_w_qkv = nrm((n_a, D_MODEL, QKV_DIM), D_MODEL)
    a_b_qkv = small((n_a, QKV_DIM))
    a_sinks = jax.random.normal(next(ks), (n_a, N_HEADS), f32) * 0.5
    a_w_o = nrm((n_a, N_HEADS * HEAD_DIM, D_MODEL), N_HEADS * HEAD_DIM)
    a_b_o = small((n_a, D_MODEL))
    b_w_in = nrm((n_b, D_MODEL, 2 * LRU_WIDTH), D_MODEL)
    b_b_in = small((n_b, 2 * LRU_WIDTH))
    b_conv_w = nrm((n_b, CONV_WIDTH, LRU_WIDTH), CONV_WIDTH)
    b_conv_b = small((n_b, LRU_WIDTH))
    b_gate_a_w = nrm((n_b, GATE_BLOCKS, GATE_BLOCK_W, GATE_BLOCK_W), GATE_BLOCK_W)
    b_gate_a_b = small((n_b, LRU_WIDTH))
    b_gate_x_w = nrm((n_b, GATE_BLOCKS, GATE_BLOCK_W, GATE_BLOCK_W), GATE_BLOCK_W)
    b_gate_x_b = small((n_b, LRU_WIDTH))
    u = jax.random.uniform(next(ks), (n_b, LRU_WIDTH), f32, 0.9, 0.999)
    base = u ** (1.0 / LRU_C)
    b_lambda = jnp.log(base) - jnp.log1p(-base)
    b_w_out = nrm((n_b, LRU_WIDTH, D_MODEL), LRU_WIDTH)
    b_b_out = small((n_b, D_MODEL))
    mlp_w_up = nrm((DEPTH, D_MODEL, D_FF), D_MODEL)
    mlp_w_down = nrm((DEPTH, D_FF, D_MODEL), D_FF)
    return {"x": x, "mix_norm": mix_norm, "mlp_norm": mlp_norm, "final_norm": final_norm,
            "a_w_qkv": a_w_qkv, "a_b_qkv": a_b_qkv, "a_sinks": a_sinks, "a_w_o": a_w_o, "a_b_o": a_b_o,
            "b_w_in": b_w_in, "b_b_in": b_b_in, "b_conv_w": b_conv_w, "b_conv_b": b_conv_b,
            "b_gate_a_w": b_gate_a_w, "b_gate_a_b": b_gate_a_b, "b_gate_x_w": b_gate_x_w,
            "b_gate_x_b": b_gate_x_b, "b_lambda": b_lambda, "b_w_out": b_w_out, "b_b_out": b_b_out,
            "mlp_w_up": mlp_w_up, "mlp_w_down": mlp_w_down}

def reference(x, mix_norm, mlp_norm, final_norm, a_w_qkv, a_b_qkv, a_sinks, a_w_o, a_b_o,
              b_w_in, b_b_in, b_conv_w, b_conv_b, b_gate_a_w, b_gate_a_b, b_gate_x_w, b_gate_x_b,
              b_lambda, b_w_out, b_b_out, mlp_w_up, mlp_w_down):
    h = x
    for layer in range(DEPTH):
        j = layer // N_MIXERS
        hn = rms_norm(h, mix_norm[layer])
        if layer % N_MIXERS == 0:
            mix = swa_sink_attention(hn, a_w_qkv[j], a_b_qkv[j], a_sinks[j], a_w_o[j], a_b_o[j])
        else:
            mix = rglru_block(hn, b_w_in[j], b_b_in[j], b_conv_w[j], b_conv_b[j],
                              b_gate_a_w[j], b_gate_a_b[j], b_gate_x_w[j], b_gate_x_b[j],
                              b_lambda[j], b_w_out[j], b_b_out[j])
        h = h + mix
        h = h + sqrelu_mlp(rms_norm(h, mlp_norm[layer]), mlp_w_up[layer], mlp_w_down[layer])
    return rms_norm(h, final_norm)


_drawn_inputs = setup_inputs


def setup_inputs(seed=0):
    import zlib

    import numpy as np

    out = dict(_drawn_inputs(seed))
    spreads = {}
    factors = {'a_b_qkv': 3.539,
     'a_sinks': 8.0,
     'a_b_o': 3.611,
     'b_b_in': 3.978,
     'b_conv_b': 3.937,
     'b_gate_a_b': 64.0,
     'b_gate_x_b': 29.208,
     'b_b_out': 8.0}
    for name, (base, spread) in spreads.items():
        noise = np.random.default_rng([zlib.crc32(name.encode()), seed]).standard_normal(out[name].shape)
        drawn = base * np.exp(spread * noise) if base else spread * noise
        out[name] = __import__('jax').numpy.asarray(drawn.astype(out[name].dtype))
    for name, factor in factors.items():
        out[name] = (out[name] * factor).astype(out[name].dtype)
    return out
```

```python
from contextlib import ExitStack, contextmanager

import numpy as np

import concourse.bass as bass
from concourse import mybir

F32 = mybir.dt.float32
F32R = mybir.dt.float32r
ALU = mybir.AluOpType
ACT = mybir.ActivationFunctionType
AX_X = mybir.AxisListType.X

PART = 128
TOK = 256
D = 2048
KT = D // PART
HEADS = 32
KV_HEADS = 4
HD = 64
D_FF = 4 * D
GROUPS = D_FF // D
GATE_BLOCKS = 8
TAPS = 4
EPS = 1e-6
NEG_BIG = -1e30 * 8.0
SCALE = HD ** -0.5

CH_KT = 4
PAIR_N = 256
CHUNKS = KT // CH_KT
SLOTS = 2 * CHUNKS

Q_QKV = (HEADS + 2 * KV_HEADS) * HD // 512
Q_WO = D // 512
Q_MLP = GROUPS * 2 * (D // 512)
Q_IN = 2 * D // 512
QB_QKV = 0
QB_WO = QB_QKV + Q_QKV
QB_MLP0 = QB_WO + Q_WO
QB_IN = QB_MLP0 + Q_MLP
QB_OUT = QB_IN + Q_IN
QB_MLP1 = QB_OUT + Q_WO
QUADS = QB_MLP1 + Q_MLP

PAIRS = D // PAIR_N
MID_ATT = 0
MID_MLP0 = MID_ATT + PAIRS
MID_LRU = MID_MLP0 + GROUPS * PAIRS
MID_MLP1 = MID_LRU + PAIRS

VEC = {}
_at = 0
for _name, _n in [("mix0", 16), ("mlp0", 16), ("mix1", 16), ("mlp1", 16), ("fin", 16), ("b_qkv", 20), ("b_o", 16),
                  ("b_in", 32), ("conv_w", 64), ("conv_b", 16), ("ga_b", 16), ("gx_b", 16), ("lam", 16),
                  ("b_out", 16), ("sinks", 64)]:
    VEC[_name] = _at
    _at += _n
VEC_N = _at


class Count:

    def __init__(self, sem):
        self.sem, self.fixed, self.moving = sem, 0, None

    def up(self, instruction):
        instruction.then_inc(self.sem, 1)
        self.fixed += 1

    @property
    def value(self):
        return self.fixed if self.moving is None else self.moving + self.fixed


@contextmanager
def repeat(eng, start, stop, count=None, per_turn=0):
    if count is None:
        with eng.Fori(start, stop) as i:
            yield i
        return
    fixed, moving = count.fixed, count.moving
    with eng.Fori(start, stop) as i:
        turn = (i - start) * per_turn if start else i * per_turn
        count.moving = turn if moving is None else moving + turn
        yield i
        assert count.fixed - fixed == per_turn, (count.fixed - fixed, per_turn)
    count.moving = moving
    count.fixed = fixed + (stop - start) * per_turn


def build(nc, x_l, vec_d, const_d, w_qkv, w_o, w_in, ga_w, gx_w, w_out, w_up, w_down, out_l):
    rows = "(kt p) n -> p kt n"
    qkv_v = w_qkv[0].rearrange(rows, p=PART)
    o_v = w_o[0].rearrange(rows, p=PART)
    in_v = w_in[0].rearrange(rows, p=PART)
    out_v = w_out[0].rearrange(rows, p=PART)
    up_v = [w_up[i].rearrange(rows, p=PART) for i in range(2)]
    down_v = [w_down[i].rearrange(rows, p=PART) for i in range(2)]
    ga_v = ga_w[0].rearrange("b (kt p) n -> p (b kt) n", p=PART)
    gx_v = gx_w[0].rearrange("b (kt p) n -> p (b kt) n", p=PART)

    ctx = ExitStack()
    with ctx:
        def sb(name, shape, dt=F32, at=ctx):
            return at.enter_context(nc.sbuf_tensor(name, shape, dt))

        def sem(name):
            return ctx.enter_context(nc.semaphore(name))

        h = sb("h", [PART, KT, TOK])
        xn = sb("xn", [PART, 2, KT, TOK], F32R)
        mid = sb("mid", [PART, 2, KT, TOK], F32R)
        w_raw = sb("w_raw", [PART, SLOTS, CH_KT, PAIR_N])
        w_hi = sb("w_hi", [PART, CHUNKS, CH_KT, PAIR_N], F32R)
        w_lo = sb("w_lo", [PART, CHUNKS, CH_KT, PAIR_N], F32R)
        half = sb("half", [PART, 2, TOK])
        u = sb("u", [PART, 2, TOK])
        v = sb("v", [PART, 2, TOK])
        sq = sb("sq", [PART, 2, TOK])
        acc = sb("acc", [PART, 2, TOK])
        rstd = sb("rstd", [PART, TOK])
        rms = sb("rms", [PART, TOK])
        vec = sb("vec", [PART, VEC_N])
        const = sb("const", [PART, 768])
        ones = sb("ones", [PART, PART])
        eps = sb("eps", [PART, 1])
        cos, sin = const[:, 0:TOK], const[:, TOK:2 * TOK]
        swap, ident = const[:, 512:640], const[:, 640:768]

        att = ExitStack()
        kpad = sb("kpad", [PART, 2, KV_HEADS, 2, 320], F32R, att)
        vcur = sb("vcur", [PART, 2, 4, 192], F32R, att)
        vraw = sb("vraw", [PART, KV_HEADS, 4, HD], F32, att)
        qz = sb("qz", [PART, 2, 4, 192], F32R, att)
        pt = sb("pt", [PART, 2, 2, 512], F32R, att)
        att.close()
        gate_hi = sb("gate_hi", [PART, 4, PAIR_N], F32R)
        gate_lo = sb("gate_lo", [PART, 4, PAIR_N], F32R)
        xc_split = sb("xc_split", [PART, 2, 2, TOK], F32R)
        gate_raw = sb("gate_raw", [PART, 4, PAIR_N])
        y = sb("y", [PART, 2, TOK])
        ys = sb("ys", [PART, 2, TOK])
        gelu = sb("gelu", [PART, 2, TOK])
        xb = sb("xb", [PART, 2, TOK + TAPS - 1])
        xc = sb("xc", [PART, 2, TOK])
        g_half = sb("g_half", [PART, 4, TOK])
        g_r = sb("g_r", [PART, 2, TOK])
        g_i = sb("g_i", [PART, 2, TOK])
        a_exp = sb("a_exp", [PART, 2, TOK])
        th = sb("th", [PART, 2, TOK])
        decay = sb("decay", [PART, 2, TOK])
        lru = sb("lru", [PART, 12, KT])
        hf = h[:, :, :].rearrange("p k t -> p (k t)")
        prob = hf[:, 0:1032]
        vt = hf[:, 1040:1680].rearrange("p (b t) -> p b t", b=2)
        qa = hf[:, 1680:2192].rearrange("p (b t) -> p b t", b=2)
        qb = hf[:, 2192:2704].rearrange("p (b t) -> p b t", b=2)
        kswap = hf[:, 2704:3216].rearrange("p (b t) -> p b t", b=2)
        stat = hf[:, 3216:3264]
        s_max, s_m, s_den, s_rden = (stat[:, 8 * i:8 * i + 8] for i in range(4))

        ps = ctx.enter_context(nc.psum_tensor("ps", [PART, 4, 512], F32))
        aux = ctx.enter_context(nc.psum_tensor("aux", [PART, 4, 512], F32))
        x0, xs, x3 = aux[:, 0, :], aux[:, 1:3, :], aux[:, 3, :]

        raw_loaded = [sem(f"raw_loaded{i}") for i in range(SLOTS)]
        vec_loaded, const_loaded = sem("vec_loaded"), sem("const_loaded")
        x_loaded = [sem(f"x_loaded{i}") for i in range(4)]
        x_again = sem("x_again")
        hi_ready, lo_ready, wts_used = sem("hi_ready"), sem("lo_ready"), sem("wts_used")
        half_copied, psum_free = sem("half_copied"), sem("psum_free")
        h_ready, xn_hi, xn_ready = sem("h_ready"), sem("xn_hi"), sem("xn_ready")
        sq_ready, acc_ready = sem("sq_ready"), sem("acc_ready")
        consts_set = sem("consts_set")
        stats_done, rms_ready = sem("stats_done"), sem("rms_ready")
        dve_step, act_step = sem("dve_step"), sem("act_step")
        relu_ready, squared = sem("relu_ready"), sem("squared")
        mid_hi, mid_ready = sem("mid_hi"), sem("mid_ready")
        zeros_set = sem("zeros_set")
        rope_in, rotated, rot_read, roped = sem("rope_in"), sem("rotated"), sem("rot_read"), sem("roped")
        kswapped, k_hi, k_ready = sem("kswapped"), sem("k_hi"), sem("k_ready")
        vt_ready, v_transposed, v_read = sem("vt_ready"), sem("v_transposed"), sem("v_read")
        vcur_hi, vcur_ready = sem("vcur_hi"), sem("vcur_ready")
        q_hi, q_ready, scored = sem("q_hi"), sem("q_ready"), sem("scored")
        shifted, exp_done, probs_ready = sem("shifted"), sem("exp_done"), sem("probs_ready")
        transposed, pt_hi, pt_ready = sem("transposed"), sem("pt_hi"), sem("pt_ready")
        att_done, att_out_hi = sem("att_done"), sem("att_out_hi")
        gate_loaded, gate_hi_ready, gate_ready = sem("gate_loaded"), sem("gate_hi_ready"), sem("gate_ready")
        gates_done, g_copied, g_summed = sem("gates_done"), sem("g_copied"), sem("g_summed")
        sig_done, decay_in, root_done = sem("sig_done"), sem("decay_in"), sem("root_done")
        y_ready, y_sq, z_ready, y_tanh = sem("y_ready"), sem("y_sq"), sem("z_ready"), sem("y_tanh")
        xc_ready, xc_hi, xc_lo = sem("xc_ready"), sem("xc_hi"), sem("xc_lo")
        lru_out, lru_hi = sem("lru_out"), sem("lru_hi")
        lam_abs, lam_exp = sem("lam_abs"), sem("lam_exp")
        hg_ready, final_ready, stored = sem("hg_ready"), sem("final_ready"), sem("stored")

        def col(name, i):
            return vec[:, bass.ds(VEC[name] + i, 1)]

        def bc2(ap):
            return ap.unsqueeze(1).to_broadcast([PART, 2, TOK])

        def h_pair(j):
            return h[:, bass.ds(j * 2, 2), :]

        block = ctx.enter_context(nc.Block())

        @block.sync
        def _(sp):
            def load(q, half_i, s, view, row_tile, column):
                if not (isinstance(q, int) and q == 0):
                    sp.wait_ge(lo_ready, (q - 1) * SLOTS + half_i * CHUNKS + s + 1)
                slot = half_i * CHUNKS + s
                sp.dma_start(w_raw[:, slot, :, :],
                             view[:, bass.ds(row_tile + s * CH_KT, CH_KT), bass.ds(column, PAIR_N)]
                             ).then_inc(raw_loaded[slot], 16)

            def load_quad(q, view, row_tile, column, column_b=None):
                for s in range(CHUNKS):
                    load(q, 0, s, view, row_tile, column)
                for s in range(CHUNKS):
                    load(q, 1, s, view, row_tile, column + PAIR_N if column_b is None else column_b)

            sp.dma_start(vec[:, :], vec_d).then_inc(vec_loaded, 16)
            for s in range(CHUNKS):
                load(0, 0, s, qkv_v, 0, HEADS * HD)
                sp.dma_start(h[:, 4 * s:4 * s + 4, :], x_l[:, 4 * s:4 * s + 4, :]).then_inc(x_loaded[s], 16)
            sp.dma_start(const[:, :], const_d).then_inc(const_loaded, 16)
            for s in range(CHUNKS):
                load(0, 1, s, qkv_v, 0, HEADS * HD + PAIR_N)
            with sp.Fori(0, Q_QKV - 1) as i:
                load_quad(i + 1, qkv_v, 0, i * 512)
            with sp.Fori(0, Q_WO) as i:
                load_quad(i + QB_WO, o_v, 0, i * 512)

            def load_mlp(base, layer):
                with sp.Fori(0, GROUPS) as g:
                    with sp.Fori(0, 4) as i:
                        load_quad(g * 8 + i + base, up_v[layer], 0, g * D + i * 512)
                    with sp.Fori(0, 4) as i:
                        load_quad(g * 8 + i + (base + 4), down_v[layer], g * KT, i * 512)

            load_mlp(QB_MLP0, 0)
            def load_lru(n):
                load_quad(n + QB_IN, in_v, 0, n * PAIR_N, n * PAIR_N + D)
                if not isinstance(n, int):
                    sp.wait_ge(gate_ready, n)
                sp.dma_start(gate_raw[:, 0:2, :], ga_v[:, bass.ds(n * 2, 2), :]).then_inc(gate_loaded, 16)
                sp.dma_start(gate_raw[:, 2:4, :], gx_v[:, bass.ds(n * 2, 2), :]).then_inc(gate_loaded, 16)

            load_lru(0)
            with sp.Fori(1, GATE_BLOCKS) as n:
                load_lru(n)
            with sp.Fori(0, Q_WO) as i:
                load_quad(i + QB_OUT, out_v, 0, i * 512)
            load_mlp(QB_MLP1, 1)
            for c in range(4):
                sp.wait_ge(final_ready, c + 1)
                sp.dma_start(out_l[:, 4 * c:4 * c + 4, :], h[:, 4 * c:4 * c + 4, :]).then_inc(stored, 16)
            sp.wait_ge(stored, 64)

        @block.gpsimd
        def _(pool):
            nc.gpsimd.memset(ones[:, :], 1.0).then_inc(consts_set, 1)
            nc.gpsimd.memset(eps[:, :], EPS).then_inc(consts_set, 1)
            for buf in (kpad[:, 0], kpad[:, 1]):
                nc.gpsimd.memset(buf.bitcast(F32), 0.0).then_inc(zeros_set, 1)
            nc.gpsimd.memset(vcur[:, :, :, :].bitcast(F32), 0.0).then_inc(zeros_set, 1)
            nc.gpsimd.memset(qz[:, :, :, :].bitcast(F32), 0.0).then_inc(zeros_set, 1)
            pool.wait_ge(mid_ready, MID_MLP0)
            pool.dma_start(h[:, :, :], x_l[:, :, :]).then_inc(x_again, 16)

        @block.scalar
        def _(act):
            step = Count(act_step)

            def split_hi(q, half_i, s):
                slot = half_i * CHUNKS + s
                act.wait_ge(raw_loaded[slot], (q + 1) * 16)
                if not (isinstance(q, int) and q == 0 and half_i == 0):
                    act.wait_ge(wts_used, (q * 2 + half_i - 1) * CHUNKS + s + 1)
                nc.scalar.activation(w_hi[:, s, :, :], w_raw[:, slot, :, :], ACT.Copy).then_inc(hi_ready, 1)

            def next_hi(q, half_i, s):
                split_hi(q, 1, s) if half_i == 0 else split_hi(q + 1, 0, s)

            def copy_half(q, half_i, bias=None):
                act.wait_ge(wts_used, (q * 2 + half_i + 1) * CHUNKS)
                if not (isinstance(q, int) and q == 0 and half_i == 0):
                    act.wait_ge(psum_free, q * 2 + half_i)
                src = ps[:, 2 * half_i:2 * half_i + 2, TOK:2 * TOK]
                if bias is None:
                    nc.scalar.activation(half[:, :, :], src, ACT.Copy).then_inc(half_copied, 1)
                    return
                name, j = bias
                nc.scalar.activation(half[:, 0, :], src[:, 0, :], ACT.Identity, bias=col(name, j * 2))
                nc.scalar.activation(half[:, 1, :], src[:, 1, :], ACT.Identity,
                                     bias=col(name, j * 2 + 1)).then_inc(half_copied, 1)

            def norm_operand(j, ready, gain):
                act.wait_ge(h_ready, ready)
                act.wait_ge(acc_ready, ready)
                nc.scalar.activation(sq[:, :, :], h_pair(j), ACT.Square).then_inc(sq_ready, 1)
                for b in range(2):
                    last = nc.scalar.activation(xn[:, 0, bass.ds(j * 2 + b, 1), :], h[:, bass.ds(j * 2 + b, 1), :],
                                                ACT.Copy, scale=col(gain, j * 2 + b))
                last.then_inc(xn_hi, 1)

            def root(n):
                act.wait_ge(stats_done, n + 1)
                nc.scalar.activation(rms[:, :], x3[:, 0:TOK], ACT.Sqrt, bias=eps[:, :], scale=1.0 / D
                                     ).then_inc(rms_ready, 1)

            def residual(q, half_i, j, bias=None, norm=None):
                copy_half(q, half_i, bias)
                if norm is not None:
                    n, gain = norm
                    norm_operand(j, j + (8 * (n - 1) + 1), gain)

            act.wait_ge(vec_loaded, 16)
            for s in range(CHUNKS):
                split_hi(0, 0, s)
                act.wait_ge(x_loaded[s], 16)
                for kt in range(4 * s, 4 * s + 4):
                    last = nc.scalar.activation(xn[:, 0, kt, :], h[:, kt, :], ACT.Copy, scale=col("mix0", kt))
                    if kt % 2:
                        last.then_inc(xn_hi, 1)
            for j in range(PAIRS):
                if j:
                    act.wait_ge(acc_ready, j)
                nc.scalar.activation(sq[:, :, :], h_pair(j), ACT.Square).then_inc(sq_ready, 1)

            def roped_hi(j):
                act.wait_ge(roped, j + 2)
                nc.scalar.activation(qz[:, 0, :, :].rearrange("p b (c t) -> p b c t", c=3)[:, :, 0:3:2, :],
                                     qa[:, :, :].rearrange("p b (t c x) -> p (b t) c x", t=2, c=2),
                                     ACT.Copy).then_inc(q_hi, 1)

            def pt_split_hi(j, b):
                act.wait_ge(transposed, j * 2 + b + 1)
                nc.scalar.activation(pt[:, 0, b, :], x3, ACT.Copy).then_inc(pt_hi, 1)

            def softmax_exp(j):
                act.wait_ge(shifted, j + 1)
                nc.scalar.activation(prob, prob, ACT.Exp).then_inc(exp_done, 1)

            def att_hi(j):
                act.wait_ge(att_done, j + 1)
                nc.scalar.activation(mid[:, 0, bass.ds(j * 2, 2), :], x0.rearrange("p (b t) -> p b t", b=2),
                                     ACT.Copy).then_inc(att_out_hi, 1)

            def vcur_split_hi(g):
                nc.scalar.activation(vcur[:, 0, :, HD:2 * HD], vraw[:, g, :, :], ACT.Copy).then_inc(vcur_hi, 1)

            for s in range(3):
                next_hi(0, 0, s)
            root(0)
            copy_half(0, 0)
            next_hi(0, 0, 3)
            next_hi(0, 1, 0)
            act.wait_ge(roped, 1)
            nc.scalar.activation(kswap[HD:PART, :, :], qa[0:HD, :, :], ACT.Copy)
            nc.scalar.activation(kswap[0:HD, :, :], qa[HD:PART, :, :], ACT.Copy).then_inc(kswapped, 1)
            act.wait_ge(zeros_set, 4)
            act.wait_ge(kswapped, 1)
            kv = kpad[:, 0, :, :, HD:HD + TOK].rearrange("p (b s) a t -> p b s a t", s=2)
            for part, side, src in ((0, 0, qa), (0, 1, kswap), (1, 1, qa), (1, 0, kswap)):
                r = slice(HD * part, HD * part + HD)
                last = nc.scalar.activation(kv[r, :, side, part, :], src[r, :, :], ACT.Copy)
            last.then_inc(k_hi, 1)
            next_hi(0, 1, 1)
            next_hi(0, 1, 2)
            copy_half(0, 1)
            next_hi(0, 1, 3)
            for s in range(3):
                next_hi(1, 0, s)
            copy_half(1, 0)
            next_hi(1, 0, 3)
            next_hi(1, 1, 0)
            roped_hi(0)
            next_hi(1, 1, 1)
            next_hi(1, 1, 2)
            softmax_exp(0)
            copy_half(1, 1)
            next_hi(1, 1, 3)

            def attention_step(q, half_i, j):
                next_hi(q, half_i, 0)
                if half_i == 0:
                    act.wait_ge(v_read, 1)
                    vcur_split_hi(q - 2)
                roped_hi(j)
                pt_split_hi(j - 1, 0)
                next_hi(q, half_i, 1)
                pt_split_hi(j - 1, 1)
                next_hi(q, half_i, 2)
                softmax_exp(j)
                att_hi(j - 1)
                copy_half(q, half_i)
                next_hi(q, half_i, 3)

            with act.Fori(2, Q_QKV) as q:
                attention_step(q, 0, q * 2 - 3)
                attention_step(q, 1, q * 2 - 2)

            q, j = QB_WO, PAIRS - 1
            next_hi(q, 0, 0)
            vcur_split_hi(KV_HEADS - 1)
            roped_hi(j)
            pt_split_hi(j - 1, 0)
            next_hi(q, 0, 1)
            pt_split_hi(j - 1, 1)
            next_hi(q, 0, 2)
            softmax_exp(j)
            att_hi(j - 1)
            pt_split_hi(j, 0)
            pt_split_hi(j, 1)
            att_hi(j)
            residual(q, 0, 0, ("b_o", 0), (1, "mlp0"))
            next_hi(q, 0, 3)

            def residual_step(q, half_i, j, bias=None, norm=None):
                for s in range(3):
                    next_hi(q, half_i, s)
                residual(q, half_i, j, bias, norm)
                next_hi(q, half_i, 3)

            residual_step(q, 1, 1, ("b_o", 1), (1, "mlp0"))
            with act.Fori(1, Q_WO) as i:
                residual_step(i + QB_WO, 0, i * 2, ("b_o", i * 2), (1, "mlp0"))
                residual_step(i + QB_WO, 1, i * 2 + 1, ("b_o", i * 2 + 1), (1, "mlp0"))

            def up_step(q, half_i, j, relus, norm=None):
                for s in range(3):
                    next_hi(q, half_i, s)
                if norm is not None:
                    root(norm)
                copy_half(q, half_i)
                act.wait_ge(relu_ready, relus + 1)
                nc.scalar.activation(mid[:, 0, bass.ds(j * 2, 2), :], u[:, :, :], ACT.Square).then_inc(mid_hi, 1)
                next_hi(q, half_i, 3)

            def mlp(base, norm, gain, relus):
                def up_quad(q, i, r, norm=None):
                    up_step(q, 0, i * 2, r, norm)
                    up_step(q, 1, i * 2 + 1, r + 1)

                up_quad(base, 0, relus, norm)
                with act.Fori(1, 4) as i:
                    up_quad(i + base, i, i * 2 + relus)
                with act.Fori(0, 4) as i:
                    residual_step(i + (base + 4), 0, i * 2)
                    residual_step(i + (base + 4), 1, i * 2 + 1)
                with act.Fori(1, GROUPS - 1) as g:
                    with act.Fori(0, 4) as i:
                        up_quad(g * 8 + i + base, i, g * 8 + i * 2 + relus)
                    with act.Fori(0, 4) as i:
                        residual_step(g * 8 + i + (base + 4), 0, i * 2)
                        residual_step(g * 8 + i + (base + 4), 1, i * 2 + 1)
                last = base + 8 * (GROUPS - 1)
                with act.Fori(0, 4) as i:
                    up_quad(i + last, i, i * 2 + (8 * (GROUPS - 1) + relus))
                return last + 4

            last = mlp(QB_MLP0, 1, "mlp0", 0)
            with act.Fori(0, 4) as i:
                residual_step(i + last, 0, i * 2, None, (2, "mix1"))
                residual_step(i + last, 1, i * 2 + 1, None, (2, "mix1"))

            def gate_sums(n):
                act.wait_ge(gates_done, n + 1)
                nc.scalar.activation(g_half[:, :, :], aux[:, :, TOK:2 * TOK], ACT.Copy).then_inc(g_copied, 1)

            def gate_sigmoids(n):
                act.wait_ge(g_summed, n + 1)
                for b in range(2):
                    nc.scalar.activation(g_r[:, b, :], g_r[:, b, :], ACT.Sigmoid, bias=col("ga_b", n * 2 + b))
                for b in range(2):
                    last = nc.scalar.activation(g_i[:, b, :], g_i[:, b, :], ACT.Sigmoid, bias=col("gx_b", n * 2 + b))
                last.then_inc(sig_done, 1)

            def decays(n):
                act.wait_ge(sig_done, n + 1)
                for b in range(2):
                    nc.scalar.activation(a_exp[:, b, :], g_r[:, b, :], ACT.Exp,
                                         scale=lru[:, 0, bass.ds(n * 2 + b, 1)])
                for b in range(2):
                    last = nc.scalar.activation(th[:, b, :], g_r[:, b, :], ACT.Tanh,
                                                scale=lru[:, 1, bass.ds(n * 2 + b, 1)])
                last.then_inc(decay_in, 1)

            def y_square(n):
                act.wait_ge(y_ready, n + 1)
                nc.scalar.activation(ys[:, :, :], y[:, :, :], ACT.Square).then_inc(y_sq, 1)

            def y_tanh_step(n):
                act.wait_ge(z_ready, n + 1)
                nc.scalar.activation(ys[:, :, :], ys[:, :, :], ACT.Tanh, scale=0.7978845608028654).then_inc(y_tanh, 1)

            def roots(n):
                act.wait_ge(decay_in, n + 1)
                nc.scalar.activation(g_r[:, :, :], th[:, :, :], ACT.Sqrt).then_inc(root_done, 1)

            def lru_split_hi(n):
                act.wait_ge(lru_out, n + 1)
                nc.scalar.activation(mid[:, 0, bass.ds(n * 2, 2), :], v[:, :, :], ACT.Copy).then_inc(lru_hi, 1)

            def gate_split_hi(n):
                act.wait_ge(gate_loaded, (n + 1) * 32)
                if not (isinstance(n, int) and n == 0):
                    act.wait_ge(gates_done, n)
                nc.scalar.activation(gate_hi[:, :, :], gate_raw[:, :, :], ACT.Copy).then_inc(gate_hi_ready, 1)

            def xc_split_hi(n):
                act.wait_ge(xc_ready, n + 1)
                nc.scalar.activation(xc_split[:, 0, :, :], xc[:, :, :], ACT.Copy).then_inc(xc_hi, 1)

            def lru_quad(q, n, first=False):
                next_hi(q, 0, 0)
                next_hi(q, 0, 1)
                if first:
                    act.wait_ge(lam_abs, 1)
                    nc.scalar.activation(lru[:, 3, :], lru[:, 2, :], ACT.Exp, scale=-1.0).then_inc(lam_exp, 1)
                else:
                    gate_sums(n - 1)
                next_hi(q, 0, 2)
                if first:
                    root(2)
                else:
                    gate_sigmoids(n - 1)
                copy_half(q, 0)
                next_hi(q, 0, 3)
                next_hi(q, 1, 0)
                gate_split_hi(n)
                y_square(n)
                if not first:
                    decays(n - 1)
                next_hi(q, 1, 1)
                y_tanh_step(n)
                if not first:
                    roots(n - 1)
                next_hi(q, 1, 2)
                if not first:
                    lru_split_hi(n - 1)
                copy_half(q, 1)
                xc_split_hi(n)
                next_hi(q, 1, 3)

            lru_quad(QB_IN, 0, True)
            with act.Fori(1, GATE_BLOCKS) as n:
                lru_quad(n + QB_IN, n)
            q, n = QB_OUT, GATE_BLOCKS - 1
            next_hi(q, 0, 0)
            next_hi(q, 0, 1)
            gate_sums(n)
            gate_sigmoids(n)
            decays(n)
            roots(n)
            lru_split_hi(n)
            next_hi(q, 0, 2)
            residual(q, 0, 0, ("b_out", 0), (3, "mlp1"))
            next_hi(q, 0, 3)
            residual_step(q, 1, 1, ("b_out", 1), (3, "mlp1"))
            with act.Fori(1, Q_WO) as i:
                residual_step(i + QB_OUT, 0, i * 2, ("b_out", i * 2), (3, "mlp1"))
                residual_step(i + QB_OUT, 1, i * 2 + 1, ("b_out", i * 2 + 1), (3, "mlp1"))

            last = mlp(QB_MLP1, 3, "mlp1", GROUPS * PAIRS)

            def final_step(q, half_i, j, more=True):
                if more:
                    for s in range(3):
                        next_hi(q, half_i, s)
                copy_half(q, half_i)
                act.wait_ge(h_ready, j + 25)
                act.wait_ge(acc_ready, j + 32)
                nc.scalar.activation(sq[:, :, :], h_pair(j), ACT.Square).then_inc(sq_ready, 1)
                act.wait_ge(sq_ready, j + 33)
                for b in range(2):
                    one = h[:, bass.ds(j * 2 + b, 1), :]
                    done = nc.scalar.activation(one, one, ACT.Copy, scale=col("fin", j * 2 + b))
                done.then_inc(hg_ready, 1)
                if more:
                    next_hi(q, half_i, 3)

            with act.Fori(0, 3) as i:
                final_step(i + last, 0, i * 2)
                final_step(i + last, 1, i * 2 + 1)
            final_step(last + 3, 0, 6)
            final_step(last + 3, 1, 7, False)
            root(4)

        @block.vector
        def _(dve):
            step = Count(dve_step)

            def then(ins):
                step.up(ins)
                dve.wait_ge(dve_step, step.value)

            def split_lo(q, half_i, s):
                slot = half_i * CHUNKS + s
                dve.wait_ge(hi_ready, (q * 2 + half_i) * CHUNKS + s + 1)
                nc.vector.tensor_tensor(w_lo[:, s, :, :], w_raw[:, slot, :, :], w_hi[:, s, :, :].bitcast(F32),
                                        ALU.subtract).then_inc(lo_ready, 1)

            def next_lo(q, half_i, s):
                split_lo(q, 1, s) if half_i == 0 else split_lo(q + 1, 0, s)

            def add_halves(q, half_i):
                dve.wait_ge(half_copied, q * 2 + half_i + 1)
                nc.vector.tensor_tensor(u[:, :, :], ps[:, 2 * half_i:2 * half_i + 2, 0:TOK], half[:, :, :],
                                        ALU.add).then_inc(psum_free, 1)
                dve.wait_ge(psum_free, q * 2 + half_i + 1)

            def sum_squares():
                return nc.vector.tensor_tensor(acc[:, :, :], acc[:, :, :], sq[:, :, :], ALU.add)

            def inverse_root(n):
                dve.wait_ge(rms_ready, n + 1)
                then(nc.vector.reciprocal(rstd[:, :], rms[:, :]))
                then(nc.vector.memset(acc[:, :, :], 0.0))

            def norm_operand(j, ready, gain):
                dve.wait_ge(xn_hi, ready + 8)
                for b in range(2):
                    last = nc.vector.scalar_tensor_tensor(
                        xn[:, 1, bass.ds(j * 2 + b, 1), :], in0=h[:, bass.ds(j * 2 + b, 1), :],
                        scalar=col(gain, j * 2 + b), in1=xn[:, 0, bass.ds(j * 2 + b, 1), :].bitcast(F32),
                        op0=ALU.mult, op1=ALU.subtract)
                last.then_inc(xn_ready, 1)
                dve.wait_ge(sq_ready, ready + 8)
                sum_squares().then_inc(acc_ready, 1)

            def residual(q, half_i, j, norm=None):
                add_halves(q, half_i)
                add = nc.vector.tensor_tensor(h_pair(j), h_pair(j), u[:, :, :], ALU.add)
                if norm is not None:
                    n, gain = norm
                    add.then_inc(h_ready, 1)
                    norm_operand(j, j + (8 * (n - 1) + 1), gain)

            def residual_step(q, half_i, j, norm=None):
                for s in range(3):
                    next_lo(q, half_i, s)
                residual(q, half_i, j, norm)
                next_lo(q, half_i, 3)

            then(nc.vector.memset(acc[:, :, :], 0.0))
            dve.wait_ge(vec_loaded, 16)
            for s in range(CHUNKS):
                split_lo(0, 0, s)
                for kt in range(4 * s, 4 * s + 4):
                    if kt % 2 == 0:
                        dve.wait_ge(xn_hi, kt // 2 + 1)
                    last = nc.vector.scalar_tensor_tensor(xn[:, 1, kt, :], in0=h[:, kt, :], scalar=col("mix0", kt),
                                                          in1=xn[:, 0, kt, :].bitcast(F32),
                                                          op0=ALU.mult, op1=ALU.subtract)
                    if kt % 2:
                        last.then_inc(xn_ready, 1)
            for j in range(PAIRS):
                dve.wait_ge(sq_ready, j + 1)
                if j:
                    dve.wait_ge(acc_ready, j)
                sum_squares().then_inc(acc_ready, 1)

            def scale_and_bias(q, half_i, tile, out_a, out_b):
                add_halves(q, half_i)
                then(nc.vector.tensor_tensor(u[:, :, :], u[:, :, :], bc2(rstd[:, :]), ALU.mult))
                nc.vector.tensor_scalar(out_a, u[:, 0, :], col(tile[0], tile[1]), None, ALU.add)
                return nc.vector.tensor_scalar(out_b, u[:, 1, :], col(tile[0], tile[1] + 1), None, ALU.add)

            def rope_input(q, half_i, j):
                scale_and_bias(q, half_i, ("b_qkv", j * 2), u[:, 0, :], u[:, 1, :]).then_inc(rope_in, 1)

            def rope(n):
                dve.wait_ge(rotated, n + 1)
                nc.vector.tensor_tensor(qb, x0.rearrange("p (b t) -> p b t", b=2), bc2(sin), ALU.mult
                                        ).then_inc(rot_read, 1)
                then(nc.vector.tensor_tensor(qa, u[:, :, :], bc2(cos), ALU.mult))
                nc.vector.tensor_tensor(qa, qa, qb, ALU.add).then_inc(roped, 1)

            def q_split_lo(j):
                dve.wait_ge(q_hi, j + 1)
                qc = qz[:, :, :, :].rearrange("p h b (c t) -> p h b c t", c=3)
                nc.vector.tensor_tensor(qc[:, 1, :, 0:3:2, :],
                                        qa[:, :, :].rearrange("p b (t c x) -> p (b t) c x", t=2, c=2),
                                        qc[:, 0, :, 0:3:2, :].bitcast(F32), ALU.subtract).then_inc(q_ready, 1)

            def softmax_shift(j):
                dve.wait_ge(scored, j + 1)
                first = xs.rearrange("p b (t a c x) -> p b t a c x", t=2, a=2, c=2)
                then(nc.vector.memset(first[0:HD, :, 0, :, 0, :], NEG_BIG))
                rows8 = xs.rearrange("p b (m k) -> p (b m) k", k=PART)
                then(nc.vector.reduce_max(s_max, rows8, AX_X))
                sinks = vec[:, bass.ds(VEC["sinks"] + j * 8, 8)]
                then(nc.vector.scalar_tensor_tensor(s_m, in0=s_max, scalar=SCALE, in1=sinks,
                                                    op0=ALU.mult, op1=ALU.max))
                nc.vector.tensor_tensor(prob[:, 1024:1032], sinks, s_m, ALU.subtract)
                nc.vector.scalar_tensor_tensor(prob[:, 0:1024].rearrange("p (m k) -> p m k", k=PART), in0=rows8,
                                               scalar=SCALE, in1=s_m.unsqueeze(2).to_broadcast([PART, 8, PART]),
                                               op0=ALU.mult, op1=ALU.subtract).then_inc(shifted, 1)

            def softmax_scale(j):
                dve.wait_ge(exp_done, j + 1)
                p8 = prob[:, 0:1024].rearrange("p (m k) -> p m k", k=PART)
                then(nc.vector.reduce_sum(s_den, p8, AX_X))
                then(nc.vector.tensor_tensor(s_den, s_den, prob[:, 1024:1032], ALU.add))
                then(nc.vector.reciprocal(s_rden, s_den))
                nc.vector.tensor_tensor(p8, p8, s_rden.unsqueeze(2).to_broadcast([PART, 8, PART]), ALU.mult
                                        ).then_inc(probs_ready, 1)

            def pt_split_lo(j, b):
                dve.wait_ge(pt_hi, j * 2 + b + 1)
                nc.vector.tensor_tensor(pt[:, 1, b, :], x3, pt[:, 0, b, :].bitcast(F32), ALU.subtract
                                        ).then_inc(pt_ready, 1)

            def att_lo(j):
                dve.wait_ge(att_out_hi, j + 1)
                nc.vector.tensor_tensor(mid[:, 1, bass.ds(j * 2, 2), :], x0.rearrange("p (b t) -> p b t", b=2),
                                        mid[:, 0, bass.ds(j * 2, 2), :].bitcast(F32), ALU.subtract
                                        ).then_inc(mid_ready, 1)

            def vcur_split_lo(g):
                dve.wait_ge(vcur_hi, g + 1)
                nc.vector.tensor_tensor(vcur[:, 1, :, HD:2 * HD], vraw[:, g, :, :],
                                        vcur[:, 0, :, HD:2 * HD].bitcast(F32), ALU.subtract
                                        ).then_inc(vcur_ready, 1)

            for s in range(3):
                next_lo(0, 0, s)
            inverse_root(0)
            rope_input(0, 0, 8)
            next_lo(0, 0, 3)
            next_lo(0, 1, 0)
            dve.wait_ge(const_loaded, 16)
            rope(0)
            then(nc.vector.memset(vt[:, :, 0:HD], 0.0))
            dve.wait_ge(k_hi, 1)
            kv = kpad[:, :, :, :, HD:HD + TOK].rearrange("p h (b s) a t -> p h b s a t", s=2)
            for part, side, src in ((0, 0, qa), (0, 1, kswap), (1, 1, qa), (1, 0, kswap)):
                r = slice(HD * part, HD * part + HD)
                last = nc.vector.tensor_tensor(kv[r, 1, :, side, part, :], src[r, :, :],
                                               kv[r, 0, :, side, part, :].bitcast(F32), ALU.subtract)
            last.then_inc(k_ready, 1)
            next_lo(0, 1, 1)
            next_lo(0, 1, 2)
            scale_and_bias(0, 1, ("b_qkv", 18), vt[:, 0, HD:HD + TOK], vt[:, 1, HD:HD + TOK]).then_inc(vt_ready, 1)
            next_lo(0, 1, 3)
            next_lo(1, 0, 0)
            next_lo(1, 0, 1)
            dve.wait_ge(v_transposed, 1)
            for b in range(2):
                last = nc.vector.tensor_copy(vraw[:, 2 * b:2 * b + 2, :, :],
                                             xs[:, b, :].rearrange("p (c k d) -> p k c d", c=4, k=2))
            last.then_inc(v_read, 1)
            next_lo(1, 0, 2)
            rope_input(1, 0, 0)
            next_lo(1, 0, 3)
            next_lo(1, 1, 0)
            rope(1)
            q_split_lo(0)
            next_lo(1, 1, 1)
            softmax_shift(0)
            next_lo(1, 1, 2)
            softmax_scale(0)
            rope_input(1, 1, 1)
            next_lo(1, 1, 3)

            def attention_step(q, half_i, j):
                next_lo(q, half_i, 0)
                if half_i == 0:
                    vcur_split_lo(q - 2)
                rope(j + 1)
                q_split_lo(j)
                pt_split_lo(j - 1, 0)
                next_lo(q, half_i, 1)
                pt_split_lo(j - 1, 1)
                softmax_shift(j)
                next_lo(q, half_i, 2)
                softmax_scale(j)
                att_lo(j - 1)
                rope_input(q, half_i, j + 1)
                next_lo(q, half_i, 3)

            with repeat(dve, 2, Q_QKV, step, 16) as q:
                attention_step(q, 0, q * 2 - 3)
                attention_step(q, 1, q * 2 - 2)

            q, j = QB_WO, PAIRS - 1
            next_lo(q, 0, 0)
            vcur_split_lo(KV_HEADS - 1)
            rope(j + 1)
            q_split_lo(j)
            pt_split_lo(j - 1, 0)
            next_lo(q, 0, 1)
            pt_split_lo(j - 1, 1)
            softmax_shift(j)
            next_lo(q, 0, 2)
            softmax_scale(j)
            att_lo(j - 1)
            pt_split_lo(j, 0)
            pt_split_lo(j, 1)
            att_lo(j)
            dve.wait_ge(x_again, 16)
            residual(q, 0, 0, (1, "mlp0"))
            next_lo(q, 0, 3)
            residual_step(q, 1, 1, (1, "mlp0"))
            with dve.Fori(1, Q_WO) as i:
                residual_step(i + QB_WO, 0, i * 2, (1, "mlp0"))
                residual_step(i + QB_WO, 1, i * 2 + 1, (1, "mlp0"))

            def up_step(q, half_i, j, relus, norm=None):
                for s in range(3):
                    next_lo(q, half_i, s)
                if norm is not None:
                    inverse_root(norm)
                add_halves(q, half_i)
                nc.vector.scalar_tensor_tensor(u[:, :, :], in0=u[:, :, :], scalar=0.0, in1=bc2(rstd[:, :]),
                                               op0=ALU.max, op1=ALU.mult).then_inc(relu_ready, 1)
                dve.wait_ge(relu_ready, relus + 1)
                nc.vector.tensor_tensor(v[:, :, :], u[:, :, :], u[:, :, :], ALU.mult).then_inc(squared, 1)
                dve.wait_ge(squared, relus + 1)
                dve.wait_ge(mid_hi, relus + 1)
                nc.vector.tensor_tensor(mid[:, 1, bass.ds(j * 2, 2), :], v[:, :, :],
                                        mid[:, 0, bass.ds(j * 2, 2), :].bitcast(F32), ALU.subtract
                                        ).then_inc(mid_ready, 1)
                next_lo(q, half_i, 3)

            def mlp(base, norm, gain, relus):
                def up_quad(q, i, r, norm=None):
                    up_step(q, 0, i * 2, r, norm)
                    up_step(q, 1, i * 2 + 1, r + 1)

                up_quad(base, 0, relus, norm)
                with dve.Fori(1, 4) as i:
                    up_quad(i + base, i, i * 2 + relus)
                with dve.Fori(0, 4) as i:
                    residual_step(i + (base + 4), 0, i * 2)
                    residual_step(i + (base + 4), 1, i * 2 + 1)
                with dve.Fori(1, GROUPS - 1) as g:
                    with dve.Fori(0, 4) as i:
                        up_quad(g * 8 + i + base, i, g * 8 + i * 2 + relus)
                    with dve.Fori(0, 4) as i:
                        residual_step(g * 8 + i + (base + 4), 0, i * 2)
                        residual_step(g * 8 + i + (base + 4), 1, i * 2 + 1)
                last = base + 8 * (GROUPS - 1)
                with dve.Fori(0, 4) as i:
                    up_quad(i + last, i, i * 2 + (8 * (GROUPS - 1) + relus))
                return last + 4

            last = mlp(QB_MLP0, 1, "mlp0", 0)
            with dve.Fori(0, 4) as i:
                residual_step(i + last, 0, i * 2, (2, "mix1"))
                residual_step(i + last, 1, i * 2 + 1, (2, "mix1"))

            def softplus_of_minus_lambda():
                lam = vec[:, VEC["lam"]:VEC["lam"] + KT]
                r = [lru[:, i, :] for i in range(12)]
                then(nc.vector.tensor_scalar(r[4], lam, -1.0, None, ALU.mult))
                nc.vector.tensor_tensor(r[2], lam, r[4], ALU.max).then_inc(lam_abs, 1)
                dve.wait_ge(lam_exp, 1)
                then(nc.vector.tensor_scalar(r[5], r[3], 2.0, None, ALU.add))
                then(nc.vector.reciprocal(r[6], r[5]))
                then(nc.vector.tensor_tensor(r[7], r[3], r[6], ALU.mult))
                then(nc.vector.tensor_tensor(r[8], r[7], r[7], ALU.mult))
                then(nc.vector.tensor_scalar(r[9], r[8], 1.0 / 17, None, ALU.mult))
                for k in (15, 13, 11, 9, 7, 5, 3):
                    then(nc.vector.scalar_tensor_tensor(r[9], in0=r[9], scalar=1.0 / k, in1=r[8],
                                                        op0=ALU.add, op1=ALU.mult))
                then(nc.vector.scalar_tensor_tensor(r[10], in0=r[9], scalar=1.0, in1=r[7],
                                                    op0=ALU.add, op1=ALU.mult))
                then(nc.vector.tensor_scalar(r[11], r[4], 0.0, 0.5, ALU.max, ALU.mult))
                then(nc.vector.tensor_tensor(r[11], r[11], r[10], ALU.add))
                nc.vector.tensor_scalar(lru[:, 0, :], r[11], -16.0, None, ALU.mult)
                then(nc.vector.tensor_scalar(lru[:, 1, :], r[11], 8.0, None, ALU.mult))

            def gate_sums(n):
                dve.wait_ge(g_copied, n + 1)
                nc.vector.tensor_tensor(g_r[:, :, :], aux[:, 0:2, 0:TOK], g_half[:, 0:2, :], ALU.add)
                nc.vector.tensor_tensor(g_i[:, :, :], aux[:, 2:4, 0:TOK], g_half[:, 2:4, :], ALU.add
                                        ).then_inc(g_summed, 1)

            def decay_terms(n):
                dve.wait_ge(decay_in, n + 1)
                then(nc.vector.tensor_scalar(a_exp[:, :, :], a_exp[:, :, :], 1.0, None, ALU.add))
                then(nc.vector.tensor_tensor(decay[:, :, :], th[:, :, :], a_exp[:, :, :], ALU.mult))
                then(nc.vector.tensor_scalar(decay[:, :, :], decay[:, :, :], -1.0, 1.0, ALU.mult, ALU.add))
                then(nc.vector.tensor_tensor(g_i[:, :, :], g_i[:, :, :], xc[:, :, :], ALU.mult))

            def recurrence(n):
                dve.wait_ge(root_done, n + 1)
                then(nc.vector.tensor_tensor(a_exp[:, :, :], g_r[:, :, :], a_exp[:, :, :], ALU.mult))
                then(nc.vector.tensor_tensor(g_i[:, :, :], g_i[:, :, :], a_exp[:, :, :], ALU.mult))
                for b in range(2):
                    ins = nc.vector.tensor_tensor_scan(v[:, b, :], decay[:, b, :], g_i[:, b, :], 0.0,
                                                       ALU.mult, ALU.add)
                then(ins)
                nc.vector.scalar_tensor_tensor(v[:, :, :], in0=v[:, :, :], scalar=0.5, in1=gelu[:, :, :],
                                               op0=ALU.mult, op1=ALU.mult).then_inc(lru_out, 1)

            def gelu_argument(n):
                dve.wait_ge(y_sq, n + 1)
                then(nc.vector.tensor_scalar(ys[:, :, :], ys[:, :, :], 0.044715, 1.0, ALU.mult, ALU.add))
                nc.vector.tensor_tensor(ys[:, :, :], ys[:, :, :], y[:, :, :], ALU.mult).then_inc(z_ready, 1)

            def gelu_product(n):
                dve.wait_ge(y_tanh, n + 1)
                if not (isinstance(n, int) and n == 0):
                    dve.wait_ge(lru_out, n)
                nc.vector.scalar_tensor_tensor(gelu[:, :, :], in0=ys[:, :, :], scalar=1.0, in1=y[:, :, :],
                                               op0=ALU.add, op1=ALU.mult)

            def lru_split_lo(n):
                dve.wait_ge(lru_hi, n + 1)
                nc.vector.tensor_tensor(mid[:, 1, bass.ds(n * 2, 2), :], v[:, :, :],
                                        mid[:, 0, bass.ds(n * 2, 2), :].bitcast(F32), ALU.subtract
                                        ).then_inc(mid_ready, 1)

            def gate_split_lo(n):
                dve.wait_ge(gate_hi_ready, n + 1)
                nc.vector.tensor_tensor(gate_lo[:, :, :], gate_raw[:, :, :], gate_hi[:, :, :].bitcast(F32),
                                        ALU.subtract).then_inc(gate_ready, 1)

            def conv(n):
                for b in range(2):
                    last = nc.vector.tensor_scalar(xc[:, b, :], xb[:, b, 0:TOK], col("conv_w", n * 2 + b),
                                                   col("conv_b", n * 2 + b), ALU.mult, ALU.add)
                then(last)
                for tap in range(1, TAPS):
                    for b in range(2):
                        last = nc.vector.scalar_tensor_tensor(
                            xc[:, b, :], in0=xb[:, b, tap:tap + TOK], scalar=col("conv_w", n * 2 + (b + tap * KT)),
                            in1=xc[:, b, :], op0=ALU.mult, op1=ALU.add)
                    if tap < TAPS - 1:
                        then(last)
                last.then_inc(xc_ready, 1)

            def lru_quad(q, n, first=False):
                next_lo(q, 0, 0)
                next_lo(q, 0, 1)
                if first:
                    softplus_of_minus_lambda()
                    then(nc.vector.memset(xb[:, :, 0:TAPS - 1], 0.0))
                else:
                    gate_sums(n - 1)
                next_lo(q, 0, 2)
                if first:
                    inverse_root(2)
                scale_and_bias(q, 0, ("b_in", n * 2), y[:, 0, :], y[:, 1, :]).then_inc(y_ready, 1)
                next_lo(q, 0, 3)
                next_lo(q, 1, 0)
                gate_split_lo(n)
                gelu_argument(n)
                if not first:
                    decay_terms(n - 1)
                next_lo(q, 1, 1)
                if not first:
                    recurrence(n - 1)
                gelu_product(n)
                next_lo(q, 1, 2)
                if not first:
                    lru_split_lo(n - 1)
                then(scale_and_bias(q, 1, ("b_in", n * 2 + KT), xb[:, 0, TAPS - 1:], xb[:, 1, TAPS - 1:]))
                conv(n)
                dve.wait_ge(xc_hi, n + 1)
                nc.vector.tensor_tensor(xc_split[:, 1, :, :], xc[:, :, :], xc_split[:, 0, :, :].bitcast(F32),
                                        ALU.subtract).then_inc(xc_lo, 1)
                next_lo(q, 1, 3)

            lru_quad(QB_IN, 0, True)
            with repeat(dve, 1, GATE_BLOCKS, step, 14) as n:
                lru_quad(n + QB_IN, n)
            q, n = QB_OUT, GATE_BLOCKS - 1
            next_lo(q, 0, 0)
            next_lo(q, 0, 1)
            gate_sums(n)
            decay_terms(n)
            recurrence(n)
            lru_split_lo(n)
            next_lo(q, 0, 2)
            residual(q, 0, 0, (3, "mlp1"))
            next_lo(q, 0, 3)
            residual_step(q, 1, 1, (3, "mlp1"))
            with dve.Fori(1, Q_WO) as i:
                residual_step(i + QB_OUT, 0, i * 2, (3, "mlp1"))
                residual_step(i + QB_OUT, 1, i * 2 + 1, (3, "mlp1"))

            last = mlp(QB_MLP1, 3, "mlp1", GROUPS * PAIRS)

            def final_step(q, half_i, j, more=True):
                if more:
                    for s in range(3):
                        next_lo(q, half_i, s)
                add_halves(q, half_i)
                nc.vector.tensor_tensor(h_pair(j), h_pair(j), u[:, :, :], ALU.add).then_inc(h_ready, 1)
                dve.wait_ge(sq_ready, j + 33)
                sum_squares().then_inc(acc_ready, 1)
                if more:
                    next_lo(q, half_i, 3)

            with dve.Fori(0, 3) as i:
                final_step(i + last, 0, i * 2)
                final_step(i + last, 1, i * 2 + 1)
            final_step(last + 3, 0, 6)
            final_step(last + 3, 1, 7, False)
            inverse_root(4)
            dve.wait_ge(hg_ready, PAIRS)
            for c in range(4):
                t4 = h[:, 4 * c:4 * c + 4, :]
                nc.vector.tensor_tensor(t4, t4, rstd[:, :].unsqueeze(1).to_broadcast([PART, 4, TOK]), ALU.mult
                                        ).then_inc(final_ready, 1)

        @block.tensor
        def _(pe):
            def products(q, half_i, s, operand, ready_sem, ready):
                pe.wait_ge(lo_ready, (q * 2 + half_i) * CHUNKS + s + 1)
                if s == 0 and not (isinstance(q, int) and q == 0):
                    pe.wait_ge(psum_free, q * 2 + half_i - 1)
                pe.wait_ge(ready_sem, ready + 2 * s + 2)
                for b in range(2):
                    bank = ps[:, 2 * half_i + b, :]
                    for k in range(CH_KT):
                        kt = s * CH_KT + k
                        cols = slice(b * PART, b * PART + PART)
                        nc.tensor.matmul(bank[:, :], w_hi[:, s, k, cols], operand[:, :, kt, :],
                                         start=kt == 0, stop=False)
                        last = nc.tensor.matmul(bank[:, TOK:2 * TOK], w_lo[:, s, k, cols], operand[:, 0, kt, :],
                                                start=False, stop=kt == KT - 1)
                last.then_inc(wts_used, 1)

            def pair(q, half_i, operand, ready_sem, ready, between=None):
                for s in range(CHUNKS):
                    products(q, half_i, s, operand, ready_sem, ready)
                    if between and s in between:
                        between[s]()

            def quad(q, operand, ready_sem, ready, between=None):
                pair(q, 0, operand, ready_sem, ready, between)
                pair(q, 1, operand, ready_sem, ready)

            def three(out, hi_w, lo_w, hi_x, lo_x, first, last):
                nc.tensor.matmul(out, hi_w, hi_x, start=first, stop=False)
                nc.tensor.matmul(out, hi_w, lo_x, start=False, stop=False)
                return nc.tensor.matmul(out, lo_w, hi_x, start=False, stop=last)

            def stats(n):
                pe.wait_ge(acc_ready, 8 * (n + 1))
                nc.tensor.matmul(x3[:, 0:TOK], ones[:, :], acc[:, 0, :], start=True, stop=False)
                nc.tensor.matmul(x3[:, 0:TOK], ones[:, :], acc[:, 1, :], start=False, stop=True
                                 ).then_inc(stats_done, 1)

            def rotate(n):
                pe.wait_ge(rope_in, n + 1)
                nc.tensor.matmul(x0, swap, u[:, :, :], start=True, stop=True).then_inc(rotated, 1)

            def transpose_v():
                pe.wait_ge(vt_ready, 1)
                for b in range(2):
                    for c in range(4):
                        last = nc.tensor.transpose(xs[:, b, c * PART:(c + 1) * PART], vt[:, b, HD * c:HD * c + PART],
                                                   ident)
                last.then_inc(v_transposed, 1)

            def scores(j, g):
                pe.wait_ge(q_ready, j + 1)
                if isinstance(j, int) and j == 0:
                    pe.wait_ge(v_read, 1)
                    pe.wait_ge(k_ready, 1)
                else:
                    pe.wait_ge(shifted, j)
                for b in range(2):
                    for t in range(2):
                        for e in range(2):
                            q_hi_t = qz[:, 0, 2 * b + t, HD * e:HD * e + PART]
                            q_lo_t = qz[:, 1, 2 * b + t, HD * e:HD * e + PART]
                            band = slice(HD * (2 * t + e), HD * (2 * t + e) + PART)
                            k_h = kpad[:, 0, bass.ds(g, 1), :, band].rearrange("p o a k -> p (o a) k")
                            k_l = kpad[:, 1, bass.ds(g, 1), :, band].rearrange("p o a k -> p (o a) k")
                            last = three(xs[:, b, t * TOK:(t + 1) * TOK], q_hi_t, q_lo_t, k_h, k_l, e == 0, e == 1)
                last.then_inc(scored, 1)

            def transpose_probs(j, b):
                pe.wait_ge(probs_ready, j + 1)
                if not (isinstance(j, int) and j == 0 and b == 0):
                    pe.wait_ge(pt_ready, j * 2 + b)
                for t in range(2):
                    for a in range(2):
                        m = 4 * b + 2 * t + a
                        at = a * TOK + t * PART
                        last = nc.tensor.transpose(x3[:, at:at + PART], prob[:, m * PART:(m + 1) * PART], ident)
                last.then_inc(transposed, 1)

            def attend(j, g):
                pe.wait_ge(pt_ready, j * 2 + 2)
                pe.wait_ge(vcur_ready, g + 1)
                pe.wait_ge(rot_read, j + 3 if not isinstance(j, int) or j < PAIRS - 2 else PAIRS + 1)
                for b in range(2):
                    for c in range(4):
                        out = x0[:, b * TOK + c * HD:b * TOK + (c + 1) * HD]
                        for a in range(2):
                            v_cols = slice(HD, 3 * HD) if a == 0 else slice(0, 2 * HD)
                            p_cols = slice(a * TOK + c * HD, a * TOK + (c + 1) * HD)
                            last = three(out, vcur[:, 0, c, v_cols], vcur[:, 1, c, v_cols],
                                         pt[:, 0, b, p_cols], pt[:, 1, b, p_cols], a == 0, a == 1)
                last.then_inc(att_done, 1)

            qkv = (xn, xn_ready, 0)
            pe.wait_ge(consts_set, 2)
            pair(0, 0, *qkv, {3: lambda: stats(0)})
            pe.wait_ge(const_loaded, 16)
            pair(0, 1, *qkv, {0: lambda: rotate(0)})
            pair(1, 0, *qkv, {0: transpose_v})
            pair(1, 1, *qkv, {0: lambda: rotate(1), 1: lambda: scores(0, 0)})

            def attention_pair(q, half_i, j, g_now, g_before, operand):
                def after0():
                    rotate(j + 1)
                    transpose_probs(j - 1, 0)

                def after1():
                    transpose_probs(j - 1, 1)
                    scores(j, g_now)

                pair(q, half_i, *operand, {0: after0, 1: after1, 2: lambda: attend(j - 1, g_before)})

            with pe.Fori(2, Q_QKV) as q:
                attention_pair(q, 0, q * 2 - 3, q - 2, q - 2, qkv)
                attention_pair(q, 1, q * 2 - 2, q - 1, q - 2, qkv)

            def after2():
                attend(PAIRS - 2, KV_HEADS - 1)
                transpose_probs(PAIRS - 1, 0)
                transpose_probs(PAIRS - 1, 1)
                attend(PAIRS - 1, KV_HEADS - 1)

            def after0():
                rotate(PAIRS)
                transpose_probs(PAIRS - 2, 0)

            def after1():
                transpose_probs(PAIRS - 2, 1)
                scores(PAIRS - 1, KV_HEADS - 1)

            att = (mid, mid_ready, MID_ATT)
            pair(QB_WO, 0, *att, {0: after0, 1: after1, 2: after2})
            pair(QB_WO, 1, *att)
            with pe.Fori(1, Q_WO) as i:
                quad(i + QB_WO, *att)

            def mlp(base, norm, mid_base):
                operand = (xn, xn_ready, 8 * norm)
                quad(base, *operand, {3: lambda: stats(norm)})
                with pe.Fori(1, 4) as i:
                    quad(i + base, *operand)
                with pe.Fori(0, 4) as i:
                    quad(i + (base + 4), mid, mid_ready, mid_base)
                with pe.Fori(1, GROUPS) as g:
                    with pe.Fori(0, 4) as i:
                        quad(g * 8 + i + base, *operand)
                    with pe.Fori(0, 4) as i:
                        quad(g * 8 + i + (base + 4), mid, mid_ready, g * PAIRS + mid_base)

            mlp(QB_MLP0, 1, MID_MLP0)

            def gates(n):
                pe.wait_ge(gate_ready, n + 1)
                pe.wait_ge(xc_lo, n + 1)
                if not (isinstance(n, int) and n == 0):
                    pe.wait_ge(g_summed, n)
                for gate in range(2):
                    for b in range(2):
                        for k in range(2):
                            cols = slice(b * PART, b * PART + PART)
                            nc.tensor.matmul(aux[:, 2 * gate + b, :], gate_hi[:, 2 * gate + k, cols],
                                             xc_split[:, :, k, :], start=k == 0, stop=False)
                            last = nc.tensor.matmul(aux[:, 2 * gate + b, TOK:2 * TOK],
                                                    gate_lo[:, 2 * gate + k, cols], xc_split[:, 0, k, :],
                                                    start=False, stop=k == 1)
                last.then_inc(gates_done, 1)

            lru_in = (xn, xn_ready, 16)
            quad(QB_IN, *lru_in, {3: lambda: stats(2)})
            with pe.Fori(1, GATE_BLOCKS) as n:
                quad(n + QB_IN, *lru_in, {1: lambda: gates(n - 1)})
            lru_done = (mid, mid_ready, MID_LRU)
            quad(QB_OUT, *lru_done, {1: lambda: gates(GATE_BLOCKS - 1)})
            with pe.Fori(1, Q_WO) as i:
                quad(i + QB_OUT, *lru_done)
            mlp(QB_MLP1, 3, MID_MLP1)
            stats(4)


def _rope_tables():
    half = HD // 2
    freqs = (np.float32(10000.0) ** (-np.arange(half, dtype=np.float32) / np.float32(half))).astype(np.float32)
    ang = np.arange(TOK, dtype=np.float32)[:, None] * freqs[None, :]
    p = np.arange(PART)
    cos = np.cos(ang).astype(np.float32).T[p % half]
    sin = np.sin(ang).astype(np.float32).T[p % half] * np.where(p % HD < half, -1.0, 1.0)[:, None]
    swap = np.zeros((PART, PART), np.float32)
    swap[p, p ^ half] = 1.0
    return np.concatenate([cos, sin, swap, np.eye(PART)], axis=1).astype(np.float32)


def _columns(a):
    return np.asarray(a).reshape(-1, PART).T


def kernel(**inputs):
    import concourse.bacc as bacc
    from concourse.bass_utils import run_bass_kernel_spmd

    a = {k: np.asarray(v) for k, v in inputs.items()}
    x_l = np.ascontiguousarray(a["x"][0].T.reshape(KT, PART, TOK).transpose(1, 0, 2))
    sinks = np.broadcast_to(a["a_sinks"][0].reshape(PAIRS, 2, 1, 2), (PAIRS, 2, 2, 2)).reshape(1, 64)
    parts = [a["mix_norm"][0], a["mlp_norm"][0], a["mix_norm"][1], a["mlp_norm"][1], a["final_norm"],
             a["a_b_qkv"][0], a["a_b_o"][0], a["b_b_in"][0], a["b_conv_w"][0].reshape(-1), a["b_conv_b"][0],
             a["b_gate_a_b"][0], a["b_gate_x_b"][0], a["b_lambda"][0], a["b_b_out"][0]]
    vec = np.ascontiguousarray(np.concatenate([_columns(p) for p in parts]
                                              + [np.broadcast_to(sinks, (PART, 64))], axis=1))
    arrays = {"x_l": x_l, "vec": vec, "const": _rope_tables()}
    for name in ("a_w_qkv", "a_w_o", "b_w_in", "b_gate_a_w", "b_gate_x_w", "b_w_out", "mlp_w_up", "mlp_w_down"):
        arrays[name] = np.ascontiguousarray(a[name])
    nc = bacc.Bacc("TRN2", target_bir_lowering=False, num_devices=1)
    arrays = {f"{n}_dram": v for n, v in arrays.items()}
    args = [nc.dram_tensor(n, v.shape, mybir.dt.from_np(v.dtype), kind="ExternalInput").ap()
            for n, v in arrays.items()]
    out = nc.dram_tensor("out_l", (PART, KT, TOK), F32, kind="ExternalOutput").ap()
    build(nc, *args, out)
    r = run_bass_kernel_spmd(nc, [arrays], core_ids=[0])
    y = r.results[0]["out_l"]
    return np.ascontiguousarray(y.transpose(1, 0, 2).reshape(D, TOK).T).reshape(1, TOK, D)
```

```python
from contextlib import ExitStack, contextmanager

import numpy as np

import concourse.bass as bass
from concourse import mybir

F32 = mybir.dt.float32
F32R = mybir.dt.float32r
ALU = mybir.AluOpType
ACT = mybir.ActivationFunctionType
AX_X = mybir.AxisListType.X

PART = 128
TOK = 256
D = 2048
KT = D // PART
HEADS = 32
KV_HEADS = 4
HD = 64
D_FF = 4 * D
GROUPS = D_FF // D
GATE_BLOCKS = 8
TAPS = 4
EPS = 1e-6
NEG_BIG = -1e30 * 8.0
SCALE = HD ** -0.5

CH_KT = 4
PAIR_N = 256
CHUNKS = KT // CH_KT
SLOTS = 2 * CHUNKS

Q_QKV = (HEADS + 2 * KV_HEADS) * HD // 512
Q_WO = D // 512
Q_MLP = GROUPS * 2 * (D // 512)
Q_IN = 2 * D // 512
QB_QKV = 0
QB_WO = QB_QKV + Q_QKV
QB_MLP0 = QB_WO + Q_WO
QB_IN = QB_MLP0 + Q_MLP
QB_OUT = QB_IN + Q_IN
QB_MLP1 = QB_OUT + Q_WO
QUADS = QB_MLP1 + Q_MLP

PAIRS = D // PAIR_N
MID_ATT = 0
MID_MLP0 = MID_ATT + PAIRS
MID_LRU = MID_MLP0 + GROUPS * PAIRS
MID_MLP1 = MID_LRU + PAIRS

VEC = {}
_at = 0
for _name, _n in [("mix0", 16), ("mlp0", 16), ("mix1", 16), ("mlp1", 16), ("fin", 16), ("b_qkv", 20), ("b_o", 16),
                  ("b_in", 32), ("conv_w", 64), ("conv_b", 16), ("ga_b", 16), ("gx_b", 16), ("lam", 16),
                  ("b_out", 16), ("sinks", 64)]:
    VEC[_name] = _at
    _at += _n
VEC_N = _at


def late_done(q):
    return q * SLOTS + 7


class Count:

    def __init__(self, sem):
        self.sem, self.fixed, self.moving = sem, 0, None

    def up(self, instruction):
        instruction.then_inc(self.sem, 1)
        self.fixed += 1

    @property
    def value(self):
        return self.fixed if self.moving is None else self.moving + self.fixed


@contextmanager
def repeat(eng, start, stop, count=None, per_turn=0):
    if count is None:
        with eng.Fori(start, stop) as i:
            yield i
        return
    fixed, moving = count.fixed, count.moving
    with eng.Fori(start, stop) as i:
        turn = (i - start) * per_turn if start else i * per_turn
        count.moving = turn if moving is None else moving + turn
        yield i
        assert count.fixed - fixed == per_turn, (count.fixed - fixed, per_turn)
    count.moving = moving
    count.fixed = fixed + (stop - start) * per_turn


def build(nc, x_l, vec_d, const_d, w_qkv, w_o, w_in, ga_w, gx_w, w_out, w_up, w_down, out_l):
    rows = "(kt p) n -> p kt n"
    qkv_v = w_qkv[0].rearrange(rows, p=PART)
    o_v = w_o[0].rearrange(rows, p=PART)
    in_v = w_in[0].rearrange(rows, p=PART)
    out_v = w_out[0].rearrange(rows, p=PART)
    up_v = [w_up[i].rearrange(rows, p=PART) for i in range(2)]
    down_v = [w_down[i].rearrange(rows, p=PART) for i in range(2)]
    ga_v = ga_w[0].rearrange("b (kt p) n -> p (b kt) n", p=PART)
    gx_v = gx_w[0].rearrange("b (kt p) n -> p (b kt) n", p=PART)

    ctx = ExitStack()
    with ctx:
        def sb(name, shape, dt=F32, at=ctx):
            return at.enter_context(nc.sbuf_tensor(name, shape, dt))

        def sem(name):
            return ctx.enter_context(nc.semaphore(name))

        h = sb("h", [PART, KT, TOK])
        xn = sb("xn", [PART, 2, KT, TOK], F32R)
        mid = sb("mid", [PART, 2, KT, TOK], F32R)
        w_raw = sb("w_raw", [PART, SLOTS, CH_KT, PAIR_N])
        w_hi = sb("w_hi", [PART, CHUNKS, CH_KT, PAIR_N], F32R)
        w_lo = sb("w_lo", [PART, CHUNKS, CH_KT, PAIR_N], F32R)
        half = sb("half", [PART, 2, TOK])
        u = sb("u", [PART, 2, TOK])
        v = sb("v", [PART, 2, TOK])
        sq = sb("sq", [PART, 2, TOK])
        acc = sb("acc", [PART, 2, TOK])
        rstd = sb("rstd", [PART, TOK])
        rms = sb("rms", [PART, TOK])
        vec = sb("vec", [PART, VEC_N])
        const = sb("const", [PART, 768])
        ones = sb("ones", [PART, PART])
        eps = sb("eps", [PART, 1])
        cos, sin = const[:, 0:TOK], const[:, TOK:2 * TOK]
        swap, ident = const[:, 512:640], const[:, 640:768]

        att = ExitStack()
        kpad = sb("kpad", [PART, 2, KV_HEADS, 2, 320], F32R, att)
        vcur = sb("vcur", [PART, 2, 4, 192], F32R, att)
        vraw = sb("vraw", [PART, KV_HEADS, 4, HD], F32, att)
        qz = sb("qz", [PART, 2, 4, 192], F32R, att)
        pt = sb("pt", [PART, 2, 2, 512], F32R, att)
        att.close()
        gate_hi = sb("gate_hi", [PART, 4, PAIR_N], F32R)
        gate_lo = sb("gate_lo", [PART, 4, PAIR_N], F32R)
        late_w = (gate_hi[:, :, :], gate_lo[:, :, :])
        xc_split = sb("xc_split", [PART, 2, 2, TOK], F32R)
        gate_raw = sb("gate_raw", [PART, 4, PAIR_N])
        y = sb("y", [PART, 2, TOK])
        ys = sb("ys", [PART, 2, TOK])
        gelu = sb("gelu", [PART, 2, 2, TOK])
        xb = sb("xb", [PART, 2, TOK + TAPS - 1])
        xc = sb("xc", [PART, 2, TOK])
        g_r = sb("g_r", [PART, 2, TOK])
        root_t = sb("root_t", [PART, 2, TOK])
        g_i = sb("g_i", [PART, 2, TOK])
        driven = sb("driven", [PART, 2, TOK])
        a_exp = sb("a_exp", [PART, 2, TOK])
        th = sb("th", [PART, 2, TOK])
        decay = sb("decay", [PART, 2, TOK])
        lru = sb("lru", [PART, 12, KT])
        hf = h[:, :, :].rearrange("p k t -> p (k t)")
        prob = hf[:, 0:1024]
        vt = hf[:, 1040:1680].rearrange("p (b t) -> p b t", b=2)
        qa = hf[:, 1680:2192].rearrange("p (b t) -> p b t", b=2)
        qb = hf[:, 2192:2704].rearrange("p (b t) -> p b t", b=2)
        kswap = hf[:, 2704:3216].rearrange("p (b t) -> p b t", b=2)
        stat = hf[:, 3216:3280]
        s_max, s_neg, s_sink, s_esink, s_sum, s_den, s_rden = (stat[:, 8 * i:8 * i + 8] for i in range(7))
        neg_sinks = hf[:, 3280:3344]

        ps = ctx.enter_context(nc.psum_tensor("ps", [PART, 4, 512], F32))
        aux = ctx.enter_context(nc.psum_tensor("aux", [PART, 4, 512], F32))
        x0, xs, x3 = aux[:, 0, :], aux[:, 1:3, :], aux[:, 3, :]

        raw_loaded = [sem(f"raw_loaded{i}") for i in range(SLOTS)]
        vec_loaded, const_loaded = sem("vec_loaded"), sem("const_loaded")
        x_loaded = [sem(f"x_loaded{i}") for i in range(4)]
        x_again = sem("x_again")
        hi_ready, lo_ready, wts_used = sem("hi_ready"), sem("lo_ready"), sem("wts_used")
        half_copied, psum_free = sem("half_copied"), sem("psum_free")
        h_ready, xn_hi, xn_ready = sem("h_ready"), sem("xn_hi"), sem("xn_ready")
        sq_ready, acc_ready = sem("sq_ready"), sem("acc_ready")
        consts_set = sem("consts_set")
        stats_done, rms_ready = sem("stats_done"), sem("rms_ready")
        dve_step, act_step = sem("dve_step"), sem("act_step")
        relu_ready, squared = sem("relu_ready"), sem("squared")
        mid_hi, mid_ready = sem("mid_hi"), sem("mid_ready")
        zeros_set = sem("zeros_set")
        rope_in, rotated, rot_read, roped = sem("rope_in"), sem("rotated"), sem("rot_read"), sem("roped")
        kswapped, k_hi, k_ready = sem("kswapped"), sem("k_hi"), sem("k_ready")
        vt_ready, v_transposed, v_read = sem("vt_ready"), sem("v_transposed"), sem("v_read")
        vcur_hi, vcur_ready = sem("vcur_hi"), sem("vcur_ready")
        q_hi, q_ready, scored = sem("q_hi"), sem("q_ready"), sem("scored")
        max_ready, exp_done, probs_ready = sem("max_ready"), sem("exp_done"), sem("probs_ready")
        transposed, pt_hi, pt_ready = sem("transposed"), sem("pt_hi"), sem("pt_ready")
        att_done, att_out_hi = sem("att_done"), sem("att_out_hi")
        gate_loaded, gate_hi_ready, gate_ready = sem("gate_loaded"), sem("gate_hi_ready"), sem("gate_ready")
        gates_done, y_scaled, gelu_ready = sem("gates_done"), sem("y_scaled"), sem("gelu_ready")
        sig_done, decay_in, root_done = sem("sig_done"), sem("decay_in"), sem("root_done")
        y_ready, y_sq, z_ready, y_tanh = sem("y_ready"), sem("y_sq"), sem("z_ready"), sem("y_tanh")
        x_scaled, xb_ready, tap_ready = sem("x_scaled"), sem("xb_ready"), sem("tap_ready")
        xc_ready, xc_hi, xc_lo = sem("xc_ready"), sem("xc_hi"), sem("xc_lo")
        scanned, lru_out, lru_hi = sem("scanned"), sem("lru_out"), sem("lru_hi")
        lam_abs, lam_exp = sem("lam_abs"), sem("lam_exp")
        hg_ready, final_ready, stored = sem("hg_ready"), sem("final_ready"), sem("stored")

        def col(name, i):
            return vec[:, bass.ds(VEC[name] + i, 1)]

        def bc2(ap):
            return ap.unsqueeze(1).to_broadcast([PART, 2, TOK])

        def h_pair(j):
            return h[:, bass.ds(j * 2, 2), :]

        block = ctx.enter_context(nc.Block())

        @block.sync
        def _(sp):
            def load(q, half_i, s, view, row_tile, column):
                if not (isinstance(q, int) and q == 0):
                    sp.wait_ge(lo_ready, (q - 1) * SLOTS + half_i * CHUNKS + s + 1)
                slot = half_i * CHUNKS + s
                sp.dma_start(w_raw[:, slot, :, :],
                             view[:, bass.ds(row_tile + s * CH_KT, CH_KT), bass.ds(column, PAIR_N)]
                             ).then_inc(raw_loaded[slot], 16)

            def load_quad(q, view, row_tile, column, column_b=None):
                for s in range(CHUNKS):
                    load(q, 0, s, view, row_tile, column)
                for s in range(CHUNKS):
                    load(q, 1, s, view, row_tile, column + PAIR_N if column_b is None else column_b)

            sp.dma_start(vec[:, :], vec_d).then_inc(vec_loaded, 16)
            for s in range(CHUNKS):
                load(0, 0, s, qkv_v, 0, HEADS * HD)
                sp.dma_start(h[:, 4 * s:4 * s + 4, :], x_l[:, 4 * s:4 * s + 4, :]).then_inc(x_loaded[s], 16)
            sp.dma_start(const[:, :], const_d).then_inc(const_loaded, 16)
            for s in range(CHUNKS):
                load(0, 1, s, qkv_v, 0, HEADS * HD + PAIR_N)
            with sp.Fori(0, Q_QKV - 1) as i:
                load_quad(i + 1, qkv_v, 0, i * 512)
            with sp.Fori(0, Q_WO) as i:
                load_quad(i + QB_WO, o_v, 0, i * 512)

            def load_mlp(base, layer):
                with sp.Fori(0, GROUPS) as g:
                    with sp.Fori(0, 4) as i:
                        load_quad(g * 8 + i + base, up_v[layer], 0, g * D + i * 512)
                    with sp.Fori(0, 4) as i:
                        load_quad(g * 8 + i + (base + 4), down_v[layer], g * KT, i * 512)

            load_mlp(QB_MLP0, 0)
            def load_lru(n):
                load_quad(n + QB_IN, in_v, 0, n * PAIR_N, n * PAIR_N + D)
                if not isinstance(n, int):
                    sp.wait_ge(gate_ready, n)
                sp.dma_start(gate_raw[:, 0:2, :], ga_v[:, bass.ds(n * 2, 2), :]).then_inc(gate_loaded, 16)
                sp.dma_start(gate_raw[:, 2:4, :], gx_v[:, bass.ds(n * 2, 2), :]).then_inc(gate_loaded, 16)

            load_lru(0)
            with sp.Fori(1, GATE_BLOCKS) as n:
                load_lru(n)
            with sp.Fori(0, Q_WO) as i:
                load_quad(i + QB_OUT, out_v, 0, i * 512)
            load_mlp(QB_MLP1, 1)
            for c in range(4):
                sp.wait_ge(final_ready, c + 1)
                sp.dma_start(out_l[:, 4 * c:4 * c + 4, :], h[:, 4 * c:4 * c + 4, :]).then_inc(stored, 16)
            sp.wait_ge(stored, 64)

        @block.gpsimd
        def _(pool):
            nc.gpsimd.memset(ones[:, :], 1.0).then_inc(consts_set, 1)
            nc.gpsimd.memset(eps[:, :], EPS).then_inc(consts_set, 1)
            for buf in (kpad[:, 0], kpad[:, 1]):
                nc.gpsimd.memset(buf.bitcast(F32), 0.0).then_inc(zeros_set, 1)
            nc.gpsimd.memset(vcur[:, :, :, :].bitcast(F32), 0.0).then_inc(zeros_set, 1)
            nc.gpsimd.memset(qz[:, :, :, :].bitcast(F32), 0.0).then_inc(zeros_set, 1)
            pool.wait_ge(mid_ready, MID_MLP0)
            pool.dma_start(h[:, :, :], x_l[:, :, :]).then_inc(x_again, 16)

        @block.scalar
        def _(act):
            step = Count(act_step)

            def split_hi(q, half_i, s, used=None):
                slot = half_i * CHUNKS + s
                act.wait_ge(raw_loaded[slot], (q + 1) * 16)
                if used is not None:
                    act.wait_ge(wts_used, used)
                elif not (isinstance(q, int) and q == 0 and half_i == 0):
                    act.wait_ge(wts_used, (q * 2 + half_i - 1) * CHUNKS + s + 1)
                nc.scalar.activation(w_hi[:, s, :, :], w_raw[:, slot, :, :], ACT.Copy).then_inc(hi_ready, 1)

            def next_hi(q, half_i, s):
                split_hi(q, 1, s) if half_i == 0 else split_hi(q + 1, 0, s)

            def copy_half(q, half_i, bias=None, done=None):
                act.wait_ge(wts_used, (q * 2 + half_i + 1) * CHUNKS if done is None else done)
                if not (isinstance(q, int) and q == 0 and half_i == 0):
                    act.wait_ge(psum_free, q * 2 + half_i)
                src = ps[:, 2 * half_i:2 * half_i + 2, TOK:2 * TOK]
                if bias is None:
                    nc.scalar.activation(half[:, :, :], src, ACT.Copy).then_inc(half_copied, 1)
                    return
                name, j = bias
                nc.scalar.activation(half[:, 0, :], src[:, 0, :], ACT.Identity, bias=col(name, j * 2))
                nc.scalar.activation(half[:, 1, :], src[:, 1, :], ACT.Identity,
                                     bias=col(name, j * 2 + 1)).then_inc(half_copied, 1)

            def late_hi(q):
                act.wait_ge(raw_loaded[SLOTS - 1], (q + 1) * 16)
                nc.scalar.activation(late_w[0], w_raw[:, SLOTS - 1, :, :], ACT.Copy).then_inc(hi_ready, 1)

            def after_late_hi(q, s):
                split_hi(q + 1, 0, s, q * SLOTS + CHUNKS + s)

            def norm_operand(j, ready, gain):
                act.wait_ge(h_ready, ready)
                act.wait_ge(acc_ready, ready)
                nc.scalar.activation(sq[:, :, :], h_pair(j), ACT.Square).then_inc(sq_ready, 1)
                for b in range(2):
                    last = nc.scalar.activation(xn[:, 0, bass.ds(j * 2 + b, 1), :], h[:, bass.ds(j * 2 + b, 1), :],
                                                ACT.Copy, scale=col(gain, j * 2 + b))
                last.then_inc(xn_hi, 1)

            def root(n):
                act.wait_ge(stats_done, n + 1)
                nc.scalar.activation(rms[:, :], x3[:, 0:TOK], ACT.Sqrt, bias=eps[:, :], scale=1.0 / D
                                     ).then_inc(rms_ready, 1)

            def residual(q, half_i, j, bias=None, norm=None, done=None):
                copy_half(q, half_i, bias, done)
                if norm is not None:
                    n, gain = norm
                    norm_operand(j, j + (8 * (n - 1) + 1), gain)

            def late_residuals(q, bias, norm):
                copy_half(q, 0, (bias, 0), late_done(q))
                after_late_hi(q, 3)
                n, gain = norm
                norm_operand(0, 8 * (n - 1) + 1, gain)
                residual(q, 1, 1, (bias, 1), norm)

            act.wait_ge(vec_loaded, 16)
            for s in range(CHUNKS):
                split_hi(0, 0, s)
                act.wait_ge(x_loaded[s], 16)
                for kt in range(4 * s, 4 * s + 4):
                    last = nc.scalar.activation(xn[:, 0, kt, :], h[:, kt, :], ACT.Copy, scale=col("mix0", kt))
                    if kt % 2:
                        last.then_inc(xn_hi, 1)
            for j in range(PAIRS):
                if j:
                    act.wait_ge(acc_ready, j)
                nc.scalar.activation(sq[:, :, :], h_pair(j), ACT.Square).then_inc(sq_ready, 1)

            def roped_hi(j):
                act.wait_ge(roped, j + 2)
                nc.scalar.activation(qz[:, 0, :, :].rearrange("p b (c t) -> p b c t", c=3)[:, :, 0:3:2, :],
                                     qa[:, :, :].rearrange("p b (t c x) -> p (b t) c x", t=2, c=2),
                                     ACT.Copy).then_inc(q_hi, 1)

            def pt_split_hi(j):
                act.wait_ge(transposed, j + 1)
                nc.scalar.activation(pt[:, 0, :, :], xs, ACT.Copy).then_inc(pt_hi, 1)

            def softmax_exp(j, b):
                act.wait_ge(max_ready, j + 1)
                if b == 0:
                    nc.scalar.activation(s_esink, s_sink, ACT.Exp)
                for m in range(4 * b, 4 * b + 4):
                    last = nc.scalar.activation(prob[:, m * PART:(m + 1) * PART],
                                                xs[:, b, (m % 4) * PART:(m % 4 + 1) * PART], ACT.Exp,
                                                bias=s_neg[:, m:m + 1], scale=SCALE, accum_out=s_sum[:, m:m + 1])
                last.then_inc(exp_done, 1)

            def att_hi(j):
                act.wait_ge(att_done, j + 1)
                nc.scalar.activation(mid[:, 0, bass.ds(j * 2, 2), :], x0.rearrange("p (b t) -> p b t", b=2),
                                     ACT.Copy).then_inc(att_out_hi, 1)

            def vcur_split_hi(g):
                nc.scalar.activation(vcur[:, 0, :, HD:2 * HD], vraw[:, g, :, :], ACT.Copy).then_inc(vcur_hi, 1)

            for s in range(3):
                next_hi(0, 0, s)
            root(0)
            copy_half(0, 0)
            next_hi(0, 0, 3)
            next_hi(0, 1, 0)
            act.wait_ge(roped, 1)
            nc.scalar.activation(kswap[HD:PART, :, :], qa[0:HD, :, :], ACT.Copy)
            nc.scalar.activation(kswap[0:HD, :, :], qa[HD:PART, :, :], ACT.Copy).then_inc(kswapped, 1)
            act.wait_ge(zeros_set, 4)
            act.wait_ge(kswapped, 1)
            kv = kpad[:, 0, :, :, HD:HD + TOK].rearrange("p (b s) a t -> p b s a t", s=2)
            for part, side, src in ((0, 0, qa), (0, 1, kswap), (1, 1, qa), (1, 0, kswap)):
                r = slice(HD * part, HD * part + HD)
                last = nc.scalar.activation(kv[r, :, side, part, :], src[r, :, :], ACT.Copy)
            last.then_inc(k_hi, 1)
            next_hi(0, 1, 1)
            next_hi(0, 1, 2)
            copy_half(0, 1)
            next_hi(0, 1, 3)
            for s in range(3):
                next_hi(1, 0, s)
            copy_half(1, 0)
            next_hi(1, 0, 3)
            next_hi(1, 1, 0)
            next_hi(1, 1, 1)
            roped_hi(0)
            next_hi(1, 1, 2)
            softmax_exp(0, 0)
            copy_half(1, 1)
            softmax_exp(0, 1)
            next_hi(1, 1, 3)

            def attention_stages(q, half_i, j):
                next_hi(q, half_i, 0)
                if half_i == 0:
                    act.wait_ge(v_read, 1)
                    vcur_split_hi(q - 2)
                next_hi(q, half_i, 1)
                pt_split_hi(j - 1)
                roped_hi(j)
                next_hi(q, half_i, 2)
                att_hi(j - 1)
                softmax_exp(j, 0)

            def attention_step(q, half_i, j):
                attention_stages(q, half_i, j)
                copy_half(q, half_i)
                softmax_exp(j, 1)
                next_hi(q, half_i, 3)

            with act.Fori(2, Q_QKV) as q:
                attention_step(q, 0, q * 2 - 3)
                attention_step(q, 1, q * 2 - 2)

            attention_stages(QB_WO, 0, PAIRS - 1)
            softmax_exp(PAIRS - 1, 1)
            late_hi(QB_WO)
            after_late_hi(QB_WO, 0)
            pt_split_hi(PAIRS - 1)
            after_late_hi(QB_WO, 1)
            att_hi(PAIRS - 1)
            after_late_hi(QB_WO, 2)
            late_residuals(QB_WO, "b_o", (1, "mlp0"))

            def residual_step(q, half_i, j, bias=None, norm=None):
                for s in range(3):
                    next_hi(q, half_i, s)
                residual(q, half_i, j, bias, norm)
                next_hi(q, half_i, 3)

            with act.Fori(1, Q_WO) as i:
                residual_step(i + QB_WO, 0, i * 2, ("b_o", i * 2), (1, "mlp0"))
                residual_step(i + QB_WO, 1, i * 2 + 1, ("b_o", i * 2 + 1), (1, "mlp0"))

            def up_step(q, half_i, j, relus, norm=None):
                for s in range(3):
                    next_hi(q, half_i, s)
                if norm is not None:
                    root(norm)
                copy_half(q, half_i)
                act.wait_ge(relu_ready, relus + 1)
                nc.scalar.activation(mid[:, 0, bass.ds(j * 2, 2), :], u[:, :, :], ACT.Square).then_inc(mid_hi, 1)
                next_hi(q, half_i, 3)

            def mlp(base, norm, gain, relus):
                def up_quad(q, i, r, norm=None):
                    up_step(q, 0, i * 2, r, norm)
                    up_step(q, 1, i * 2 + 1, r + 1)

                up_quad(base, 0, relus, norm)
                with act.Fori(1, 4) as i:
                    up_quad(i + base, i, i * 2 + relus)
                with act.Fori(0, 4) as i:
                    residual_step(i + (base + 4), 0, i * 2)
                    residual_step(i + (base + 4), 1, i * 2 + 1)
                with act.Fori(1, GROUPS - 1) as g:
                    with act.Fori(0, 4) as i:
                        up_quad(g * 8 + i + base, i, g * 8 + i * 2 + relus)
                    with act.Fori(0, 4) as i:
                        residual_step(g * 8 + i + (base + 4), 0, i * 2)
                        residual_step(g * 8 + i + (base + 4), 1, i * 2 + 1)
                last = base + 8 * (GROUPS - 1)
                with act.Fori(0, 4) as i:
                    up_quad(i + last, i, i * 2 + (8 * (GROUPS - 1) + relus))
                return last + 4

            last = mlp(QB_MLP0, 1, "mlp0", 0)
            with act.Fori(0, 4) as i:
                residual_step(i + last, 0, i * 2, None, (2, "mix1"))
                residual_step(i + last, 1, i * 2 + 1, None, (2, "mix1"))

            def gate_sigmoids(n):
                act.wait_ge(gates_done, n + 1)
                for b in range(2):
                    nc.scalar.activation(g_r[:, b, :], aux[:, 0, b * TOK:(b + 1) * TOK], ACT.Sigmoid,
                                         bias=col("ga_b", n * 2 + b))
                for b in range(2):
                    last = nc.scalar.activation(g_i[:, b, :], aux[:, 1, b * TOK:(b + 1) * TOK], ACT.Sigmoid,
                                                bias=col("gx_b", n * 2 + b))
                last.then_inc(sig_done, 1)

            def decay_tanh(n):
                act.wait_ge(sig_done, n + 1)
                for b in range(2):
                    nc.scalar.activation(th[:, b, :], g_r[:, b, :], ACT.Tanh,
                                         scale=lru[:, 1, bass.ds(n * 2 + b, 1)])

            def decay_exp(n):
                for b in range(2):
                    last = nc.scalar.activation(a_exp[:, b, :], g_r[:, b, :], ACT.Exp,
                                                scale=lru[:, 0, bass.ds(n * 2 + b, 1)])
                last.then_inc(decay_in, 1)

            def y_bias_and_square(n):
                act.wait_ge(y_scaled, n + 1)
                if not (isinstance(n, int) and n == 0):
                    act.wait_ge(gelu_ready, n)
                for b in range(2):
                    last = nc.scalar.activation(y[:, b, :], u[:, b, :], ACT.Identity, bias=col("b_in", n * 2 + b))
                last.then_inc(y_ready, 1)
                act.wait_ge(y_ready, n + 1)
                nc.scalar.activation(ys[:, :, :], y[:, :, :], ACT.Square, scale=0.044715 ** 0.5).then_inc(y_sq, 1)

            def y_tanh_step(n):
                act.wait_ge(z_ready, n + 1)
                nc.scalar.activation(ys[:, :, :], ys[:, :, :], ACT.Tanh, scale=0.7978845608028654).then_inc(y_tanh, 1)

            def roots(n):
                act.wait_ge(decay_in, n + 1)
                nc.scalar.activation(root_t[:, :, :], th[:, :, :], ACT.Sqrt).then_inc(root_done, 1)

            def lru_split_hi(n):
                act.wait_ge(lru_out, n + 1)
                nc.scalar.activation(mid[:, 0, bass.ds(n * 2, 2), :], v[:, :, :], ACT.Copy).then_inc(lru_hi, 1)

            def gate_split_hi(n):
                act.wait_ge(gate_loaded, (n + 1) * 32)
                if not (isinstance(n, int) and n == 0):
                    act.wait_ge(gates_done, n)
                nc.scalar.activation(gate_hi[:, :, :], gate_raw[:, :, :], ACT.Copy).then_inc(gate_hi_ready, 1)

            def conv_first_tap(n):
                act.wait_ge(x_scaled, n + 1)
                for b in range(2):
                    last = nc.scalar.activation(xb[:, b, TAPS - 1:], u[:, b, :], ACT.Identity,
                                                bias=col("b_in", n * 2 + (KT + b)))
                last.then_inc(xb_ready, 1)
                act.wait_ge(xb_ready, n + 1)
                for b in range(2):
                    last = nc.scalar.activation(xc[:, b, :], xb[:, b, 0:TOK], ACT.Identity,
                                                bias=col("conv_b", n * 2 + b), scale=col("conv_w", n * 2 + b))
                last.then_inc(tap_ready, 1)

            def xc_split_hi(n):
                act.wait_ge(xc_ready, n + 1)
                nc.scalar.activation(xc_split[:, 0, :, :], xc[:, :, :], ACT.Copy).then_inc(xc_hi, 1)

            def lru_quad(q, n, before, recur):
                if before:
                    conv_first_tap(n - 1)
                next_hi(q, 0, 0)
                if recur:
                    roots(n - 2)
                if isinstance(n, int) and n == 0:
                    act.wait_ge(lam_abs, 1)
                    nc.scalar.activation(lru[:, 3, :], lru[:, 2, :], ACT.Exp, scale=-1.0).then_inc(lam_exp, 1)
                    root(2)
                next_hi(q, 0, 1)
                if before:
                    xc_split_hi(n - 1)
                next_hi(q, 0, 2)
                copy_half(q, 0)
                next_hi(q, 0, 3)
                y_bias_and_square(n)
                next_hi(q, 1, 0)
                if before:
                    gate_sigmoids(n - 1)
                y_tanh_step(n)
                gate_split_hi(n)
                if before:
                    decay_tanh(n - 1)
                if recur:
                    lru_split_hi(n - 2)
                next_hi(q, 1, 1)
                if before:
                    decay_exp(n - 1)
                next_hi(q, 1, 2)
                copy_half(q, 1)
                next_hi(q, 1, 3)

            lru_quad(QB_IN, 0, False, False)
            lru_quad(QB_IN + 1, 1, True, False)
            with act.Fori(2, GATE_BLOCKS) as n:
                lru_quad(n + QB_IN, n, True, True)
            q, n = QB_OUT, GATE_BLOCKS - 1
            next_hi(q, 0, 0)
            conv_first_tap(n)
            xc_split_hi(n)
            roots(n - 1)
            next_hi(q, 0, 1)
            next_hi(q, 0, 2)
            gate_sigmoids(n)
            decay_tanh(n)
            lru_split_hi(n - 1)
            decay_exp(n)
            roots(n)
            late_hi(q)
            after_late_hi(q, 0)
            lru_split_hi(n)
            after_late_hi(q, 1)
            after_late_hi(q, 2)
            late_residuals(q, "b_out", (3, "mlp1"))
            with act.Fori(1, Q_WO) as i:
                residual_step(i + QB_OUT, 0, i * 2, ("b_out", i * 2), (3, "mlp1"))
                residual_step(i + QB_OUT, 1, i * 2 + 1, ("b_out", i * 2 + 1), (3, "mlp1"))

            last = mlp(QB_MLP1, 3, "mlp1", GROUPS * PAIRS)

            def final_step(q, half_i, j, more=True):
                if more:
                    for s in range(3):
                        next_hi(q, half_i, s)
                copy_half(q, half_i)
                act.wait_ge(h_ready, j + 25)
                act.wait_ge(acc_ready, j + 32)
                nc.scalar.activation(sq[:, :, :], h_pair(j), ACT.Square).then_inc(sq_ready, 1)
                act.wait_ge(sq_ready, j + 33)
                for b in range(2):
                    one = h[:, bass.ds(j * 2 + b, 1), :]
                    done = nc.scalar.activation(one, one, ACT.Copy, scale=col("fin", j * 2 + b))
                done.then_inc(hg_ready, 1)
                if more:
                    next_hi(q, half_i, 3)

            with act.Fori(0, 3) as i:
                final_step(i + last, 0, i * 2)
                final_step(i + last, 1, i * 2 + 1)
            final_step(last + 3, 0, 6)
            nc.scalar.activation(rms[:, 0:1], eps[:, :], ACT.Sqrt)
            final_step(last + 3, 1, 7, False)
            root(4)

        @block.vector
        def _(dve):
            step = Count(dve_step)

            def then(ins):
                step.up(ins)
                dve.wait_ge(dve_step, step.value)

            def split_lo(q, half_i, s):
                slot = half_i * CHUNKS + s
                dve.wait_ge(hi_ready, (q * 2 + half_i) * CHUNKS + s + 1)
                nc.vector.tensor_tensor(w_lo[:, s, :, :], w_raw[:, slot, :, :], w_hi[:, s, :, :].bitcast(F32),
                                        ALU.subtract).then_inc(lo_ready, 1)

            def late_lo(q):
                dve.wait_ge(hi_ready, (q + 1) * SLOTS)
                nc.vector.tensor_tensor(late_w[1], w_raw[:, SLOTS - 1, :, :], late_w[0].bitcast(F32), ALU.subtract
                                        ).then_inc(lo_ready, 1)

            def next_lo(q, half_i, s):
                split_lo(q, 1, s) if half_i == 0 else split_lo(q + 1, 0, s)

            def add_halves(q, half_i):
                dve.wait_ge(half_copied, q * 2 + half_i + 1)
                nc.vector.tensor_tensor(u[:, :, :], ps[:, 2 * half_i:2 * half_i + 2, 0:TOK], half[:, :, :],
                                        ALU.add).then_inc(psum_free, 1)
                dve.wait_ge(psum_free, q * 2 + half_i + 1)

            def sum_squares():
                return nc.vector.tensor_tensor(acc[:, :, :], acc[:, :, :], sq[:, :, :], ALU.add)

            def inverse_root(n):
                dve.wait_ge(rms_ready, n + 1)
                then(nc.vector.reciprocal(rstd[:, :], rms[:, :]))
                then(nc.vector.memset(acc[:, :, :], 0.0))

            def norm_operand(j, ready, gain):
                dve.wait_ge(xn_hi, ready + 8)
                for b in range(2):
                    last = nc.vector.scalar_tensor_tensor(
                        xn[:, 1, bass.ds(j * 2 + b, 1), :], in0=h[:, bass.ds(j * 2 + b, 1), :],
                        scalar=col(gain, j * 2 + b), in1=xn[:, 0, bass.ds(j * 2 + b, 1), :].bitcast(F32),
                        op0=ALU.mult, op1=ALU.subtract)
                last.then_inc(xn_ready, 1)
                dve.wait_ge(sq_ready, ready + 8)
                sum_squares().then_inc(acc_ready, 1)

            def residual(q, half_i, j, norm=None):
                add_halves(q, half_i)
                add = nc.vector.tensor_tensor(h_pair(j), h_pair(j), u[:, :, :], ALU.add)
                if norm is not None:
                    n, gain = norm
                    add.then_inc(h_ready, 1)
                    norm_operand(j, j + (8 * (n - 1) + 1), gain)

            def residual_step(q, half_i, j, norm=None):
                for s in range(3):
                    next_lo(q, half_i, s)
                residual(q, half_i, j, norm)
                next_lo(q, half_i, 3)

            def late_residuals(q, norm):
                add_halves(q, 0)
                nc.vector.tensor_tensor(h_pair(0), h_pair(0), u[:, :, :], ALU.add).then_inc(h_ready, 1)
                next_lo(q, 1, 3)
                n, gain = norm
                norm_operand(0, 8 * (n - 1) + 1, gain)
                residual(q, 1, 1, norm)

            then(nc.vector.memset(acc[:, :, :], 0.0))
            dve.wait_ge(vec_loaded, 16)
            for s in range(CHUNKS):
                split_lo(0, 0, s)
                for kt in range(4 * s, 4 * s + 4):
                    if kt % 2 == 0:
                        dve.wait_ge(xn_hi, kt // 2 + 1)
                    last = nc.vector.scalar_tensor_tensor(xn[:, 1, kt, :], in0=h[:, kt, :], scalar=col("mix0", kt),
                                                          in1=xn[:, 0, kt, :].bitcast(F32),
                                                          op0=ALU.mult, op1=ALU.subtract)
                    if kt % 2:
                        last.then_inc(xn_ready, 1)
            for j in range(PAIRS):
                dve.wait_ge(sq_ready, j + 1)
                if j:
                    dve.wait_ge(acc_ready, j)
                sum_squares().then_inc(acc_ready, 1)

            def scale_and_bias(q, half_i, tile, out_a, out_b):
                add_halves(q, half_i)
                then(nc.vector.tensor_tensor(u[:, :, :], u[:, :, :], bc2(rstd[:, :]), ALU.mult))
                nc.vector.tensor_scalar(out_a, u[:, 0, :], col(tile[0], tile[1]), None, ALU.add)
                return nc.vector.tensor_scalar(out_b, u[:, 1, :], col(tile[0], tile[1] + 1), None, ALU.add)

            def rope_input(q, half_i, j):
                scale_and_bias(q, half_i, ("b_qkv", j * 2), u[:, 0, :], u[:, 1, :]).then_inc(rope_in, 1)

            def rope(n):
                dve.wait_ge(rotated, n + 1)
                nc.vector.tensor_tensor(qb, x3.rearrange("p (b t) -> p b t", b=2), bc2(sin), ALU.mult
                                        ).then_inc(rot_read, 1)
                then(nc.vector.tensor_tensor(qa, u[:, :, :], bc2(cos), ALU.mult))
                nc.vector.tensor_tensor(qa, qa, qb, ALU.add).then_inc(roped, 1)

            def q_split_lo(j):
                dve.wait_ge(q_hi, j + 1)
                qc = qz[:, :, :, :].rearrange("p h b (c t) -> p h b c t", c=3)
                nc.vector.tensor_tensor(qc[:, 1, :, 0:3:2, :],
                                        qa[:, :, :].rearrange("p b (t c x) -> p (b t) c x", t=2, c=2),
                                        qc[:, 0, :, 0:3:2, :].bitcast(F32), ALU.subtract).then_inc(q_ready, 1)

            def softmax_max(j):
                dve.wait_ge(scored, j + 1)
                first = xs.rearrange("p b (t a c x) -> p b t a c x", t=2, a=2, c=2)
                then(nc.vector.memset(first[0:HD, :, 0, :, 0, :], NEG_BIG))
                then(nc.vector.reduce_max(s_max, xs.rearrange("p b (m k) -> p (b m) k", k=PART), AX_X))
                then(nc.vector.scalar_tensor_tensor(s_neg, in0=s_max, scalar=-SCALE,
                                                    in1=neg_sinks[:, bass.ds(j * 8, 8)], op0=ALU.mult, op1=ALU.min))
                nc.vector.tensor_tensor(s_sink, vec[:, bass.ds(VEC["sinks"] + j * 8, 8)], s_neg, ALU.add
                                        ).then_inc(max_ready, 1)

            def softmax_scale(j):
                dve.wait_ge(exp_done, j * 2 + 2)
                p8 = prob.rearrange("p (m k) -> p m k", k=PART)
                then(nc.vector.tensor_tensor(s_den, s_sum, s_esink, ALU.add))
                then(nc.vector.reciprocal(s_rden, s_den))
                nc.vector.tensor_tensor(p8, p8, s_rden.unsqueeze(2).to_broadcast([PART, 8, PART]), ALU.mult
                                        ).then_inc(probs_ready, 1)

            def pt_split_lo(j):
                dve.wait_ge(pt_hi, j + 1)
                nc.vector.tensor_tensor(pt[:, 1, :, :], xs, pt[:, 0, :, :].bitcast(F32), ALU.subtract
                                        ).then_inc(pt_ready, 1)

            def att_lo(j):
                dve.wait_ge(att_out_hi, j + 1)
                nc.vector.tensor_tensor(mid[:, 1, bass.ds(j * 2, 2), :], x0.rearrange("p (b t) -> p b t", b=2),
                                        mid[:, 0, bass.ds(j * 2, 2), :].bitcast(F32), ALU.subtract
                                        ).then_inc(mid_ready, 1)

            def vcur_split_lo(g):
                dve.wait_ge(vcur_hi, g + 1)
                nc.vector.tensor_tensor(vcur[:, 1, :, HD:2 * HD], vraw[:, g, :, :],
                                        vcur[:, 0, :, HD:2 * HD].bitcast(F32), ALU.subtract
                                        ).then_inc(vcur_ready, 1)

            for s in range(3):
                next_lo(0, 0, s)
            inverse_root(0)
            rope_input(0, 0, 8)
            next_lo(0, 0, 3)
            next_lo(0, 1, 0)
            dve.wait_ge(const_loaded, 16)
            rope(0)
            then(nc.vector.memset(vt[:, :, 0:HD], 0.0))
            dve.wait_ge(k_hi, 1)
            kv = kpad[:, :, :, :, HD:HD + TOK].rearrange("p h (b s) a t -> p h b s a t", s=2)
            for part, side, src in ((0, 0, qa), (0, 1, kswap), (1, 1, qa), (1, 0, kswap)):
                r = slice(HD * part, HD * part + HD)
                last = nc.vector.tensor_tensor(kv[r, 1, :, side, part, :], src[r, :, :],
                                               kv[r, 0, :, side, part, :].bitcast(F32), ALU.subtract)
            last.then_inc(k_ready, 1)
            next_lo(0, 1, 1)
            next_lo(0, 1, 2)
            scale_and_bias(0, 1, ("b_qkv", 18), vt[:, 0, HD:HD + TOK], vt[:, 1, HD:HD + TOK]).then_inc(vt_ready, 1)
            next_lo(0, 1, 3)
            next_lo(1, 0, 0)
            next_lo(1, 0, 1)
            dve.wait_ge(v_transposed, 1)
            for b in range(2):
                last = nc.vector.tensor_copy(vraw[:, 2 * b:2 * b + 2, :, :],
                                             xs[:, b, :].rearrange("p (c k d) -> p k c d", c=4, k=2))
            last.then_inc(v_read, 1)
            next_lo(1, 0, 2)
            rope_input(1, 0, 0)
            next_lo(1, 0, 3)
            then(nc.vector.tensor_scalar(neg_sinks, vec[:, VEC["sinks"]:VEC["sinks"] + 64], -1.0, None, ALU.mult))
            next_lo(1, 1, 0)
            next_lo(1, 1, 1)
            rope(1)
            q_split_lo(0)
            next_lo(1, 1, 2)
            softmax_max(0)
            rope_input(1, 1, 1)
            softmax_scale(0)
            next_lo(1, 1, 3)

            def attention_stages(q, half_i, j):
                next_lo(q, half_i, 0)
                if half_i == 0:
                    vcur_split_lo(q - 2)
                next_lo(q, half_i, 1)
                pt_split_lo(j - 1)
                rope(j + 1)
                q_split_lo(j)
                next_lo(q, half_i, 2)
                att_lo(j - 1)
                softmax_max(j)

            def attention_step(q, half_i, j):
                attention_stages(q, half_i, j)
                rope_input(q, half_i, j + 1)
                softmax_scale(j)
                next_lo(q, half_i, 3)

            with repeat(dve, 2, Q_QKV, step, 14) as q:
                attention_step(q, 0, q * 2 - 3)
                attention_step(q, 1, q * 2 - 2)

            attention_stages(QB_WO, 0, PAIRS - 1)
            softmax_scale(PAIRS - 1)
            late_lo(QB_WO)
            next_lo(QB_WO, 1, 0)
            pt_split_lo(PAIRS - 1)
            next_lo(QB_WO, 1, 1)
            att_lo(PAIRS - 1)
            next_lo(QB_WO, 1, 2)
            dve.wait_ge(x_again, 16)
            late_residuals(QB_WO, (1, "mlp0"))
            with dve.Fori(1, Q_WO) as i:
                residual_step(i + QB_WO, 0, i * 2, (1, "mlp0"))
                residual_step(i + QB_WO, 1, i * 2 + 1, (1, "mlp0"))

            def up_step(q, half_i, j, relus, norm=None):
                for s in range(3):
                    next_lo(q, half_i, s)
                if norm is not None:
                    inverse_root(norm)
                add_halves(q, half_i)
                nc.vector.scalar_tensor_tensor(u[:, :, :], in0=u[:, :, :], scalar=0.0, in1=bc2(rstd[:, :]),
                                               op0=ALU.max, op1=ALU.mult).then_inc(relu_ready, 1)
                dve.wait_ge(relu_ready, relus + 1)
                nc.vector.tensor_tensor(v[:, :, :], u[:, :, :], u[:, :, :], ALU.mult).then_inc(squared, 1)
                dve.wait_ge(squared, relus + 1)
                dve.wait_ge(mid_hi, relus + 1)
                nc.vector.tensor_tensor(mid[:, 1, bass.ds(j * 2, 2), :], v[:, :, :],
                                        mid[:, 0, bass.ds(j * 2, 2), :].bitcast(F32), ALU.subtract
                                        ).then_inc(mid_ready, 1)
                next_lo(q, half_i, 3)

            def mlp(base, norm, gain, relus):
                def up_quad(q, i, r, norm=None):
                    up_step(q, 0, i * 2, r, norm)
                    up_step(q, 1, i * 2 + 1, r + 1)

                up_quad(base, 0, relus, norm)
                with dve.Fori(1, 4) as i:
                    up_quad(i + base, i, i * 2 + relus)
                with dve.Fori(0, 4) as i:
                    residual_step(i + (base + 4), 0, i * 2)
                    residual_step(i + (base + 4), 1, i * 2 + 1)
                with dve.Fori(1, GROUPS - 1) as g:
                    with dve.Fori(0, 4) as i:
                        up_quad(g * 8 + i + base, i, g * 8 + i * 2 + relus)
                    with dve.Fori(0, 4) as i:
                        residual_step(g * 8 + i + (base + 4), 0, i * 2)
                        residual_step(g * 8 + i + (base + 4), 1, i * 2 + 1)
                last = base + 8 * (GROUPS - 1)
                with dve.Fori(0, 4) as i:
                    up_quad(i + last, i, i * 2 + (8 * (GROUPS - 1) + relus))
                return last + 4

            last = mlp(QB_MLP0, 1, "mlp0", 0)
            with dve.Fori(0, 4) as i:
                residual_step(i + last, 0, i * 2, (2, "mix1"))
                residual_step(i + last, 1, i * 2 + 1, (2, "mix1"))

            def softplus_of_minus_lambda():
                lam = vec[:, VEC["lam"]:VEC["lam"] + KT]
                r = [lru[:, i, :] for i in range(12)]
                then(nc.vector.tensor_scalar(r[4], lam, -1.0, None, ALU.mult))
                nc.vector.tensor_tensor(r[2], lam, r[4], ALU.max).then_inc(lam_abs, 1)
                dve.wait_ge(lam_exp, 1)
                then(nc.vector.tensor_scalar(r[5], r[3], 2.0, None, ALU.add))
                then(nc.vector.reciprocal(r[6], r[5]))
                then(nc.vector.tensor_tensor(r[7], r[3], r[6], ALU.mult))
                then(nc.vector.tensor_tensor(r[8], r[7], r[7], ALU.mult))
                then(nc.vector.tensor_scalar(r[9], r[8], 1.0 / 17, None, ALU.mult))
                for k in (15, 13, 11, 9, 7, 5, 3):
                    then(nc.vector.scalar_tensor_tensor(r[9], in0=r[9], scalar=1.0 / k, in1=r[8],
                                                        op0=ALU.add, op1=ALU.mult))
                then(nc.vector.scalar_tensor_tensor(r[10], in0=r[9], scalar=1.0, in1=r[7],
                                                    op0=ALU.add, op1=ALU.mult))
                then(nc.vector.tensor_scalar(r[11], r[4], 0.0, 0.5, ALU.max, ALU.mult))
                then(nc.vector.tensor_tensor(r[11], r[11], r[10], ALU.add))
                nc.vector.tensor_scalar(lru[:, 0, :], r[11], -16.0, None, ALU.mult)
                then(nc.vector.tensor_scalar(lru[:, 1, :], r[11], 8.0, None, ALU.mult))

            def gate_input(n):
                dve.wait_ge(sig_done, n + 1)
                then(nc.vector.tensor_tensor(driven[:, :, :], g_i[:, :, :], xc[:, :, :], ALU.mult))

            def decay_terms(n):
                dve.wait_ge(decay_in, n + 1)
                then(nc.vector.scalar_tensor_tensor(decay[:, :, :], in0=a_exp[:, :, :], scalar=1.0,
                                                    in1=th[:, :, :], op0=ALU.add, op1=ALU.mult))
                then(nc.vector.tensor_scalar(decay[:, :, :], decay[:, :, :], -1.0, 1.0, ALU.mult, ALU.add))

            def recurrence(n):
                dve.wait_ge(root_done, n + 1)
                then(nc.vector.scalar_tensor_tensor(a_exp[:, :, :], in0=a_exp[:, :, :], scalar=1.0,
                                                    in1=root_t[:, :, :], op0=ALU.add, op1=ALU.mult))
                then(nc.vector.tensor_tensor(driven[:, :, :], driven[:, :, :], a_exp[:, :, :], ALU.mult))
                for b in range(2):
                    ins = nc.vector.tensor_tensor_scan(v[:, b, :], decay[:, b, :], driven[:, b, :], 0.0,
                                                       ALU.mult, ALU.add)
                ins.then_inc(scanned, 1)

            def recurrent_output(n, parity):
                dve.wait_ge(scanned, n + 1)
                nc.vector.scalar_tensor_tensor(v[:, :, :], in0=v[:, :, :], scalar=0.5, in1=gelu[:, parity, :, :],
                                               op0=ALU.mult, op1=ALU.mult).then_inc(lru_out, 1)

            def gelu_argument(n):
                dve.wait_ge(y_sq, n + 1)
                nc.vector.scalar_tensor_tensor(ys[:, :, :], in0=ys[:, :, :], scalar=1.0, in1=y[:, :, :],
                                               op0=ALU.add, op1=ALU.mult).then_inc(z_ready, 1)

            def gelu_product(n, parity, reused):
                dve.wait_ge(y_tanh, n + 1)
                if reused:
                    dve.wait_ge(lru_out, n - 1)
                nc.vector.scalar_tensor_tensor(gelu[:, parity, :, :], in0=ys[:, :, :], scalar=1.0, in1=y[:, :, :],
                                               op0=ALU.add, op1=ALU.mult).then_inc(gelu_ready, 1)

            def lru_split_lo(n):
                dve.wait_ge(lru_hi, n + 1)
                nc.vector.tensor_tensor(mid[:, 1, bass.ds(n * 2, 2), :], v[:, :, :],
                                        mid[:, 0, bass.ds(n * 2, 2), :].bitcast(F32), ALU.subtract
                                        ).then_inc(mid_ready, 1)

            def gate_split_lo(n):
                dve.wait_ge(gate_hi_ready, n + 1)
                nc.vector.tensor_tensor(gate_lo[:, :, :], gate_raw[:, :, :], gate_hi[:, :, :].bitcast(F32),
                                        ALU.subtract).then_inc(gate_ready, 1)

            def scaled(q, half_i):
                add_halves(q, half_i)
                return nc.vector.tensor_tensor(u[:, :, :], u[:, :, :], bc2(rstd[:, :]), ALU.mult)

            def conv(n):
                dve.wait_ge(tap_ready, n + 1)
                for tap in range(1, TAPS):
                    for b in range(2):
                        last = nc.vector.scalar_tensor_tensor(
                            xc[:, b, :], in0=xb[:, b, tap:tap + TOK], scalar=col("conv_w", n * 2 + (b + tap * KT)),
                            in1=xc[:, b, :], op0=ALU.mult, op1=ALU.add)
                    if tap < TAPS - 1:
                        then(last)
                last.then_inc(xc_ready, 1)

            def xc_split_lo(n):
                dve.wait_ge(xc_hi, n + 1)
                nc.vector.tensor_tensor(xc_split[:, 1, :, :], xc[:, :, :], xc_split[:, 0, :, :].bitcast(F32),
                                        ALU.subtract).then_inc(xc_lo, 1)

            def lru_quad(q, n, parity, before, recur):
                if recur:
                    decay_terms(n - 2)
                if before:
                    conv(n - 1)
                next_lo(q, 0, 0)
                if isinstance(n, int) and n == 0:
                    softplus_of_minus_lambda()
                    then(nc.vector.memset(xb[:, :, 0:TAPS - 1], 0.0))
                    inverse_root(2)
                if before:
                    xc_split_lo(n - 1)
                next_lo(q, 0, 1)
                next_lo(q, 0, 2)
                scaled(q, 0).then_inc(y_scaled, 1)
                next_lo(q, 0, 3)
                gelu_argument(n)
                next_lo(q, 1, 0)
                if recur:
                    recurrence(n - 2)
                    recurrent_output(n - 2, parity)
                if before:
                    gate_input(n - 1)
                gate_split_lo(n)
                gelu_product(n, parity, recur)
                next_lo(q, 1, 1)
                if recur:
                    lru_split_lo(n - 2)
                next_lo(q, 1, 2)
                scaled(q, 1).then_inc(x_scaled, 1)
                next_lo(q, 1, 3)

            lru_quad(QB_IN, 0, 0, False, False)
            lru_quad(QB_IN + 1, 1, 1, True, False)
            with repeat(dve, 1, GATE_BLOCKS // 2, step, 14) as two:
                lru_quad(two * 2 + QB_IN, two * 2, 0, True, True)
                lru_quad(two * 2 + (QB_IN + 1), two * 2 + 1, 1, True, True)
            q, n = QB_OUT, GATE_BLOCKS - 1
            next_lo(q, 0, 0)
            decay_terms(n - 1)
            conv(n)
            xc_split_lo(n)
            recurrence(n - 1)
            recurrent_output(n - 1, 0)
            next_lo(q, 0, 1)
            next_lo(q, 0, 2)
            gate_input(n)
            lru_split_lo(n - 1)
            decay_terms(n)
            recurrence(n)
            recurrent_output(n, 1)
            late_lo(q)
            lru_split_lo(n)
            for s in range(3):
                next_lo(q, 1, s)
            late_residuals(q, (3, "mlp1"))
            with dve.Fori(1, Q_WO) as i:
                residual_step(i + QB_OUT, 0, i * 2, (3, "mlp1"))
                residual_step(i + QB_OUT, 1, i * 2 + 1, (3, "mlp1"))

            last = mlp(QB_MLP1, 3, "mlp1", GROUPS * PAIRS)

            def final_step(q, half_i, j, more=True):
                if more:
                    for s in range(3):
                        next_lo(q, half_i, s)
                add_halves(q, half_i)
                nc.vector.tensor_tensor(h_pair(j), h_pair(j), u[:, :, :], ALU.add).then_inc(h_ready, 1)
                dve.wait_ge(sq_ready, j + 33)
                sum_squares().then_inc(acc_ready, 1)
                if more:
                    next_lo(q, half_i, 3)

            with dve.Fori(0, 3) as i:
                final_step(i + last, 0, i * 2)
                final_step(i + last, 1, i * 2 + 1)
            final_step(last + 3, 0, 6)
            final_step(last + 3, 1, 7, False)
            inverse_root(4)
            dve.wait_ge(hg_ready, PAIRS)
            for c in range(4):
                t4 = h[:, 4 * c:4 * c + 4, :]
                nc.vector.tensor_tensor(t4, t4, rstd[:, :].unsqueeze(1).to_broadcast([PART, 4, TOK]), ALU.mult
                                        ).then_inc(final_ready, 1)

        @block.tensor
        def _(pe):
            def products(q, half_i, s, operand, ready_sem, ready, late=False):
                pe.wait_ge(lo_ready, (q * 2 + half_i) * CHUNKS + s + 1)
                if s == 0 and not (isinstance(q, int) and q == 0):
                    pe.wait_ge(psum_free, q * 2 + half_i - 1)
                pe.wait_ge(ready_sem, ready + 2 * s + 2)
                hi, lo = late_w if late else (w_hi[:, s], w_lo[:, s])
                for b in range(2):
                    bank = ps[:, 2 * half_i + b, :]
                    for k in range(CH_KT):
                        kt = s * CH_KT + k
                        cols = slice(b * PART, b * PART + PART)
                        nc.tensor.matmul(bank[:, :], hi[:, k, cols], operand[:, :, kt, :],
                                         start=kt == 0, stop=False)
                        last = nc.tensor.matmul(bank[:, TOK:2 * TOK], lo[:, k, cols], operand[:, 0, kt, :],
                                                start=False, stop=kt == KT - 1)
                last.then_inc(wts_used, 1)

            def pair(q, half_i, operand, ready_sem, ready, between=None):
                for s in range(CHUNKS):
                    products(q, half_i, s, operand, ready_sem, ready)
                    if between and s in between:
                        between[s]()

            def quad(q, operand, ready_sem, ready, between=None, between_b=None):
                pair(q, 0, operand, ready_sem, ready, between)
                pair(q, 1, operand, ready_sem, ready, between_b)

            def three(out, hi_w, lo_w, hi_x, lo_x, first, last):
                nc.tensor.matmul(out, hi_w, hi_x, start=first, stop=False)
                nc.tensor.matmul(out, hi_w, lo_x, start=False, stop=False)
                return nc.tensor.matmul(out, lo_w, hi_x, start=False, stop=last)

            def stats(n):
                pe.wait_ge(acc_ready, 8 * (n + 1))
                nc.tensor.matmul(x3[:, 0:TOK], ones[:, :], acc[:, 0, :], start=True, stop=False)
                nc.tensor.matmul(x3[:, 0:TOK], ones[:, :], acc[:, 1, :], start=False, stop=True
                                 ).then_inc(stats_done, 1)

            def rotate(n):
                pe.wait_ge(rope_in, n + 1)
                nc.tensor.matmul(x3, swap, u[:, :, :], start=True, stop=True).then_inc(rotated, 1)

            def transpose_v():
                pe.wait_ge(vt_ready, 1)
                for b in range(2):
                    for c in range(4):
                        last = nc.tensor.transpose(xs[:, b, c * PART:(c + 1) * PART], vt[:, b, HD * c:HD * c + PART],
                                                   ident)
                last.then_inc(v_transposed, 1)

            def scores(j, g):
                pe.wait_ge(q_ready, j + 1)
                if isinstance(j, int) and j == 0:
                    pe.wait_ge(v_read, 1)
                    pe.wait_ge(k_ready, 1)
                else:
                    pe.wait_ge(pt_ready, j)
                for b in range(2):
                    for t in range(2):
                        for e in range(2):
                            q_hi_t = qz[:, 0, 2 * b + t, HD * e:HD * e + PART]
                            q_lo_t = qz[:, 1, 2 * b + t, HD * e:HD * e + PART]
                            band = slice(HD * (2 * t + e), HD * (2 * t + e) + PART)
                            k_h = kpad[:, 0, bass.ds(g, 1), :, band].rearrange("p o a k -> p (o a) k")
                            k_l = kpad[:, 1, bass.ds(g, 1), :, band].rearrange("p o a k -> p (o a) k")
                            last = three(xs[:, b, t * TOK:(t + 1) * TOK], q_hi_t, q_lo_t, k_h, k_l, e == 0, e == 1)
                last.then_inc(scored, 1)

            def transpose_probs(j):
                pe.wait_ge(probs_ready, j + 1)
                for b in range(2):
                    for t in range(2):
                        for a in range(2):
                            m = 4 * b + 2 * t + a
                            at = a * TOK + t * PART
                            last = nc.tensor.transpose(xs[:, b, at:at + PART], prob[:, m * PART:(m + 1) * PART], ident)
                last.then_inc(transposed, 1)

            def attend(j, g):
                pe.wait_ge(pt_ready, j + 1)
                pe.wait_ge(vcur_ready, g + 1)
                if not (isinstance(j, int) and j == 0):
                    pe.wait_ge(mid_ready, j)
                for c in range(4):
                    out = x0.rearrange("p (b t) -> p b t", b=2)[:, :, c * HD:(c + 1) * HD]
                    for a in range(2):
                        v_cols = slice(HD, 3 * HD) if a == 0 else slice(0, 2 * HD)
                        p_cols = slice(a * TOK + c * HD, a * TOK + (c + 1) * HD)
                        last = three(out, vcur[:, 0, c, v_cols], vcur[:, 1, c, v_cols],
                                     pt[:, 0, :, p_cols], pt[:, 1, :, p_cols], a == 0, a == 1)
                last.then_inc(att_done, 1)

            qkv = (xn, xn_ready, 0)
            pe.wait_ge(consts_set, 2)
            pair(0, 0, *qkv, {3: lambda: stats(0)})
            pe.wait_ge(const_loaded, 16)
            pair(0, 1, *qkv, {1: lambda: rotate(0)})
            pair(1, 0, *qkv, {1: transpose_v})

            def after1(j, with_before):
                if with_before:
                    transpose_probs(j - 1)
                rotate(j + 1)

            def after2(j, g, g_before):
                if g_before is not None:
                    attend(j - 1, g_before)
                scores(j, g)

            def attention_pair(q, half_i, j, g, g_before):
                pair(q, half_i, *qkv, {1: lambda: after1(j, g_before is not None), 2: lambda: after2(j, g, g_before)})

            attention_pair(1, 1, 0, 0, None)
            with pe.Fori(2, Q_QKV) as q:
                attention_pair(q, 0, q * 2 - 3, q - 2, q - 2)
                attention_pair(q, 1, q * 2 - 2, q - 1, q - 2)

            def late_quad(q, operand, between):
                for half_i, s in ((0, 0), (0, 1), (0, 2), (1, 0), (1, 1), (1, 2), (0, 3), (1, 3)):
                    products(q, half_i, s, *operand, late=(half_i, s) == (1, 3))
                    if (half_i, s) in between:
                        between[half_i, s]()

            def last_heads():
                transpose_probs(PAIRS - 1)
                attend(PAIRS - 1, KV_HEADS - 1)

            att = (mid, mid_ready, MID_ATT)
            late_quad(QB_WO, att, {(0, 1): lambda: after1(PAIRS - 1, True),
                                   (0, 2): lambda: after2(PAIRS - 1, KV_HEADS - 1, KV_HEADS - 1),
                                   (1, 2): last_heads})
            with pe.Fori(1, Q_WO) as i:
                quad(i + QB_WO, *att)

            def mlp(base, norm, mid_base):
                operand = (xn, xn_ready, 8 * norm)
                quad(base, *operand, {3: lambda: stats(norm)})
                with pe.Fori(1, 4) as i:
                    quad(i + base, *operand)
                with pe.Fori(0, 4) as i:
                    quad(i + (base + 4), mid, mid_ready, mid_base)
                with pe.Fori(1, GROUPS) as g:
                    with pe.Fori(0, 4) as i:
                        quad(g * 8 + i + base, *operand)
                    with pe.Fori(0, 4) as i:
                        quad(g * 8 + i + (base + 4), mid, mid_ready, g * PAIRS + mid_base)

            mlp(QB_MLP0, 1, MID_MLP0)

            def gates(n):
                pe.wait_ge(gate_ready, n + 1)
                pe.wait_ge(xc_lo, n + 1)
                if not (isinstance(n, int) and n == 0):
                    pe.wait_ge(sig_done, n)
                for gate in range(2):
                    for b in range(2):
                        for k in range(2):
                            cols = slice(b * PART, b * PART + PART)
                            last = three(aux[:, gate, b * TOK:(b + 1) * TOK], gate_hi[:, 2 * gate + k, cols],
                                         gate_lo[:, 2 * gate + k, cols], xc_split[:, 0, k, :], xc_split[:, 1, k, :],
                                         k == 0, k == 1)
                last.then_inc(gates_done, 1)

            lru_in = (xn, xn_ready, 16)
            quad(QB_IN, *lru_in, {3: lambda: stats(2)})
            with pe.Fori(1, GATE_BLOCKS) as n:
                quad(n + QB_IN, *lru_in, None, {0: lambda: gates(n - 1)})
            lru_done = (mid, mid_ready, MID_LRU)
            late_quad(QB_OUT, lru_done, {(1, 0): lambda: gates(GATE_BLOCKS - 1)})
            with pe.Fori(1, Q_WO) as i:
                quad(i + QB_OUT, *lru_done)
            mlp(QB_MLP1, 3, MID_MLP1)
            stats(4)


def _rope_tables():
    half = HD // 2
    freqs = (np.float32(10000.0) ** (-np.arange(half, dtype=np.float32) / np.float32(half))).astype(np.float32)
    ang = np.arange(TOK, dtype=np.float32)[:, None] * freqs[None, :]
    p = np.arange(PART)
    cos = np.cos(ang).astype(np.float32).T[p % half]
    sin = np.sin(ang).astype(np.float32).T[p % half] * np.where(p % HD < half, -1.0, 1.0)[:, None]
    swap = np.zeros((PART, PART), np.float32)
    swap[p, p ^ half] = 1.0
    return np.concatenate([cos, sin, swap, np.eye(PART)], axis=1).astype(np.float32)


def _columns(a):
    return np.asarray(a).reshape(-1, PART).T


def kernel(**inputs):
    import concourse.bacc as bacc
    from concourse.bass_utils import run_bass_kernel_spmd

    a = {k: np.asarray(v) for k, v in inputs.items()}
    x_l = np.ascontiguousarray(a["x"][0].T.reshape(KT, PART, TOK).transpose(1, 0, 2))
    sinks = np.broadcast_to(a["a_sinks"][0].reshape(PAIRS, 2, 1, 2), (PAIRS, 2, 2, 2)).reshape(1, 64)
    parts = [a["mix_norm"][0], a["mlp_norm"][0], a["mix_norm"][1], a["mlp_norm"][1], a["final_norm"],
             a["a_b_qkv"][0], a["a_b_o"][0], a["b_b_in"][0], a["b_conv_w"][0].reshape(-1), a["b_conv_b"][0],
             a["b_gate_a_b"][0], a["b_gate_x_b"][0], a["b_lambda"][0], a["b_b_out"][0]]
    vec = np.ascontiguousarray(np.concatenate([_columns(p) for p in parts]
                                              + [np.broadcast_to(sinks, (PART, 64))], axis=1))
    arrays = {"x_l": x_l, "vec": vec, "const": _rope_tables()}
    for name in ("a_w_qkv", "a_w_o", "b_w_in", "b_gate_a_w", "b_gate_x_w", "b_w_out", "mlp_w_up", "mlp_w_down"):
        arrays[name] = np.ascontiguousarray(a[name])
    nc = bacc.Bacc("TRN2", target_bir_lowering=False, num_devices=1)
    arrays = {f"{n}_dram": v for n, v in arrays.items()}
    args = [nc.dram_tensor(n, v.shape, mybir.dt.from_np(v.dtype), kind="ExternalInput").ap()
            for n, v in arrays.items()]
    out = nc.dram_tensor("out_l", (PART, KT, TOK), F32, kind="ExternalOutput").ap()
    build(nc, *args, out)
    r = run_bass_kernel_spmd(nc, [arrays], core_ids=[0])
    y = r.results[0]["out_l"]
    return np.ascontiguousarray(y.transpose(1, 0, 2).reshape(D, TOK).T).reshape(1, TOK, D)
```

```python
from contextlib import ExitStack, contextmanager

import numpy as np

import concourse.bass as bass
from concourse import mybir

F32 = mybir.dt.float32
F32R = mybir.dt.float32r
ALU = mybir.AluOpType
ACT = mybir.ActivationFunctionType
AX_X = mybir.AxisListType.X

PART = 128
TOK = 256
D = 2048
KT = D // PART
HEADS = 32
KV_HEADS = 4
HD = 64
D_FF = 4 * D
GROUPS = D_FF // D
GATE_BLOCKS = 8
TAPS = 4
EPS = 1e-6
NEG_BIG = -1e30 * 8.0
SCALE = HD ** -0.5

CH_KT = 4
PAIR_N = 256
CHUNKS = KT // CH_KT
WARM_UP = 17
SLOTS = 2 * CHUNKS

Q_QKV = (HEADS + 2 * KV_HEADS) * HD // 512
Q_WO = D // 512
Q_MLP = GROUPS * 2 * (D // 512)
Q_IN = 2 * D // 512
QB_QKV = 0
QB_WO = QB_QKV + Q_QKV
QB_MLP0 = QB_WO + Q_WO
QB_IN = QB_MLP0 + Q_MLP
QB_OUT = QB_IN + Q_IN
QB_MLP1 = QB_OUT + Q_WO
QUADS = QB_MLP1 + Q_MLP

PAIRS = D // PAIR_N
MID_ATT = 0
MID_MLP0 = MID_ATT + PAIRS
MID_LRU = MID_MLP0 + GROUPS * PAIRS
MID_MLP1 = MID_LRU + PAIRS

VEC = {}
_at = 0
for _name, _n in [("mix0", 16), ("mlp0", 16), ("mix1", 16), ("mlp1", 16), ("fin", 16), ("b_qkv", 20), ("b_o", 16),
                  ("b_in", 32), ("conv_w", 64), ("conv_b", 16), ("ga_b", 16), ("gx_b", 16), ("lam", 16),
                  ("b_out", 16), ("sinks", 64)]:
    VEC[_name] = _at
    _at += _n
VEC_N = _at


def late_done(q):
    return q * SLOTS + 7


class Count:

    def __init__(self, sem):
        self.sem, self.fixed, self.moving = sem, 0, None

    def up(self, instruction):
        instruction.then_inc(self.sem, 1)
        self.fixed += 1

    @property
    def value(self):
        return self.fixed if self.moving is None else self.moving + self.fixed


@contextmanager
def repeat(eng, start, stop, count=None, per_turn=0):
    if count is None:
        with eng.Fori(start, stop) as i:
            yield i
        return
    fixed, moving = count.fixed, count.moving
    with eng.Fori(start, stop) as i:
        turn = (i - start) * per_turn if start else i * per_turn
        count.moving = turn if moving is None else moving + turn
        yield i
        assert count.fixed - fixed == per_turn, (count.fixed - fixed, per_turn)
    count.moving = moving
    count.fixed = fixed + (stop - start) * per_turn


def build(nc, x_l, vec_d, const_d, w_qkv, w_o, w_in, ga_w, gx_w, w_out, w_up, w_down, out_l):
    rows = "(kt p) n -> p kt n"
    qkv_v = w_qkv[0].rearrange(rows, p=PART)
    o_v = w_o[0].rearrange(rows, p=PART)
    in_v = w_in[0].rearrange(rows, p=PART)
    out_v = w_out[0].rearrange(rows, p=PART)
    up_v = [w_up[i].rearrange(rows, p=PART) for i in range(2)]
    down_v = [w_down[i].rearrange(rows, p=PART) for i in range(2)]
    ga_v = ga_w[0].rearrange("b (kt p) n -> p (b kt) n", p=PART)
    gx_v = gx_w[0].rearrange("b (kt p) n -> p (b kt) n", p=PART)

    ctx = ExitStack()
    with ctx:
        def sb(name, shape, dt=F32, at=ctx):
            return at.enter_context(nc.sbuf_tensor(name, shape, dt))

        def sem(name):
            return ctx.enter_context(nc.semaphore(name))

        h = sb("h", [PART, KT, TOK])
        xn = sb("xn", [PART, 2, KT, TOK], F32R)
        mid = sb("mid", [PART, 2, KT, TOK], F32R)
        w_raw = sb("w_raw", [PART, SLOTS, CH_KT, PAIR_N])
        w_hi = sb("w_hi", [PART, CHUNKS, CH_KT, PAIR_N], F32R)
        w_lo = sb("w_lo", [PART, CHUNKS, CH_KT, PAIR_N], F32R)
        half = sb("half", [PART, 2, TOK])
        u = sb("u", [PART, 2, TOK])
        v = sb("v", [PART, 2, TOK])
        sq = sb("sq", [PART, 2, TOK])
        acc = sb("acc", [PART, 2, TOK])
        rstd = sb("rstd", [PART, TOK])
        rms = sb("rms", [PART, TOK])
        vec = sb("vec", [PART, VEC_N])
        const = sb("const", [PART, 768])
        ones = sb("ones", [PART, PART])
        eps = sb("eps", [PART, 1])
        cos, sin = const[:, 0:TOK], const[:, TOK:2 * TOK]
        swap, ident = const[:, 512:640], const[:, 640:768]

        att = ExitStack()
        kpad = sb("kpad", [PART, 2, KV_HEADS, 2, 320], F32R, att)
        vcur = sb("vcur", [PART, 2, 4, 192], F32R, att)
        before = ExitStack()
        first_sq = sb("first_sq", [PART, KT, TOK], F32, before)
        before.close()
        vraw = sb("vraw", [PART, KV_HEADS, 4, HD], F32, att)
        qz = sb("qz", [PART, 2, 4, 192], F32R, att)
        pt = sb("pt", [PART, 2, 2, 512], F32R, att)
        att.close()
        gate_hi = sb("gate_hi", [PART, 4, PAIR_N], F32R)
        gate_lo = sb("gate_lo", [PART, 4, PAIR_N], F32R)
        late_w = (gate_hi[:, :, :], gate_lo[:, :, :])
        xc_split = sb("xc_split", [PART, 2, 2, TOK], F32R)
        gate_raw = sb("gate_raw", [PART, 4, PAIR_N])
        y = sb("y", [PART, 2, TOK])
        ys = sb("ys", [PART, 2, TOK])
        gelu = sb("gelu", [PART, 2, TOK])
        xb = sb("xb", [PART, 2, TOK + TAPS - 1])
        xc = sb("xc", [PART, 2, TOK])
        g_r = sb("g_r", [PART, 2, TOK])
        root_t = sb("root_t", [PART, 2, TOK])
        g_i = sb("g_i", [PART, 2, TOK])
        driven = sb("driven", [PART, 2, TOK])
        a_exp = sb("a_exp", [PART, 2, TOK])
        th = sb("th", [PART, 2, TOK])
        decay = sb("decay", [PART, 2, TOK])
        lru = sb("lru", [PART, 12, KT])
        hf = h[:, :, :].rearrange("p k t -> p (k t)")
        places = {}
        at = 0
        for name, size in (("vt", 640), ("kswap", 512), ("prob", 1024), ("qa", 512), ("qb", 512), ("stat", 56),
                           ("neg_sinks", 64)):
            places[name] = hf[:, at:at + size]
            at += size
        vt, kswap, qa, qb = (places[name].rearrange("p (b t) -> p b t", b=2) for name in ("vt", "kswap", "qa", "qb"))
        prob, neg_sinks = places["prob"], places["neg_sinks"]
        s_max, s_neg, s_sink, s_esink, s_sum, s_den, s_rden = (places["stat"][:, 8 * i:8 * i + 8] for i in range(7))

        ps = ctx.enter_context(nc.psum_tensor("ps", [PART, 4, 512], F32))
        aux = ctx.enter_context(nc.psum_tensor("aux", [PART, 4, 512], F32))
        x0, xs, x3 = aux[:, 0, :], aux[:, 1:3, :], aux[:, 3, :]

        raw_loaded = [sem(f"raw_loaded{i}") for i in range(SLOTS)]
        gain_loaded, vec_loaded, const_loaded = sem("gain_loaded"), sem("vec_loaded"), sem("const_loaded")
        x_loaded = [sem(f"x_loaded{i}") for i in range(4)]
        x_again, x_again_rest = sem("x_again"), sem("x_again_rest")
        hi_ready, lo_ready, wts_used = sem("hi_ready"), sem("lo_ready"), sem("wts_used")
        half_copied, psum_free = sem("half_copied"), sem("psum_free")
        h_ready, xn_hi, xn_ready = sem("h_ready"), sem("xn_hi"), sem("xn_ready")
        sq_ready, acc_ready = sem("sq_ready"), sem("acc_ready")
        consts_set = sem("consts_set")
        stats_done, rms_ready = sem("stats_done"), sem("rms_ready")
        dve_step = sem("dve_step")
        relu_ready, squared = sem("relu_ready"), sem("squared")
        mid_hi, mid_ready = sem("mid_hi"), sem("mid_ready")
        zeros_set = sem("zeros_set")
        qkv_scaled, cos_done = sem("qkv_scaled"), sem("cos_done")
        rope_in, rotated, rot_read, roped = sem("rope_in"), sem("rotated"), sem("rot_read"), sem("roped")
        kswapped, k_hi, k_ready = sem("kswapped"), sem("k_hi"), sem("k_ready")
        vt_ready, v_transposed, v_read = sem("vt_ready"), sem("v_transposed"), sem("v_read")
        vcur_hi, vcur_ready = sem("vcur_hi"), sem("vcur_ready")
        q_hi, q_ready, scored = sem("q_hi"), sem("q_ready"), sem("scored")
        max_ready, exp_done, probs_ready = sem("max_ready"), sem("exp_done"), sem("probs_ready")
        transposed, pt_hi, pt_ready = sem("transposed"), sem("pt_hi"), sem("pt_ready")
        att_done, att_out_hi = sem("att_done"), sem("att_out_hi")
        gate_loaded, gate_hi_ready, gate_ready = sem("gate_loaded"), sem("gate_hi_ready"), sem("gate_ready")
        gates_done, y_scaled, gelu_ready = sem("gates_done"), sem("y_scaled"), sem("gelu_ready")
        sig_done, decay_in, root_done = sem("sig_done"), sem("decay_in"), sem("root_done")
        y_ready, y_sq, z_ready, y_tanh = sem("y_ready"), sem("y_sq"), sem("z_ready"), sem("y_tanh")
        x_scaled, xb_ready, tap_ready = sem("x_scaled"), sem("xb_ready"), sem("tap_ready")
        xc_ready, xc_hi, xc_lo = sem("xc_ready"), sem("xc_hi"), sem("xc_lo")
        scanned, lru_out, lru_hi = sem("scanned"), sem("lru_out"), sem("lru_hi")
        lam_abs, lam_exp = sem("lam_abs"), sem("lam_exp")
        hg_ready, final_ready, stored = sem("hg_ready"), sem("final_ready"), sem("stored")

        def col(name, i):
            return vec[:, bass.ds(VEC[name] + i, 1)]

        def bc2(ap):
            return ap.unsqueeze(1).to_broadcast([PART, 2, TOK])

        def h_pair(j):
            return h[:, bass.ds(j * 2, 2), :]

        block = ctx.enter_context(nc.Block())

        @block.sync
        def _(sp):
            def load(q, half_i, s, view, row_tile, column):
                if not (isinstance(q, int) and q == 0):
                    sp.wait_ge(lo_ready, (q - 1) * SLOTS + half_i * CHUNKS + s + 1)
                slot = half_i * CHUNKS + s
                sp.dma_start(w_raw[:, slot, :, :],
                             view[:, bass.ds(row_tile + s * CH_KT, CH_KT), bass.ds(column, PAIR_N)]
                             ).then_inc(raw_loaded[slot], 16)

            def load_quad(q, view, row_tile, column):
                for s in range(CHUNKS):
                    load(q, 0, s, view, row_tile, column)
                for s in range(CHUNKS):
                    load(q, 1, s, view, row_tile, column + PAIR_N)

            sp.dma_start(vec[:, 0:KT], vec_d[:, 0:KT]).then_inc(gain_loaded, 16)
            for s in range(CHUNKS):
                load(0, 0, s, qkv_v, 0, HEADS * HD)
                sp.dma_start(h[:, 4 * s:4 * s + 4, :], x_l[:, 4 * s:4 * s + 4, :]).then_inc(x_loaded[s], 16)
            for s in range(CHUNKS):
                load(0, 1, s, qkv_v, 0, HEADS * HD + PAIR_N)
            sp.dma_start(vec[:, KT:VEC_N], vec_d[:, KT:VEC_N]).then_inc(vec_loaded, 16)
            sp.dma_start(const[:, :], const_d).then_inc(const_loaded, 16)
            with sp.Fori(0, Q_QKV - 1) as i:
                load_quad(i + 1, qkv_v, 0, i * 512)
            with sp.Fori(0, Q_WO) as i:
                load_quad(i + QB_WO, o_v, 0, i * 512)

            def load_mlp(base, layer):
                with sp.Fori(0, GROUPS) as g:
                    with sp.Fori(0, 4) as i:
                        load_quad(g * 8 + i + base, up_v[layer], 0, g * D + i * 512)
                    with sp.Fori(0, 4) as i:
                        load_quad(g * 8 + i + (base + 4), down_v[layer], g * KT, i * 512)

            load_mlp(QB_MLP0, 0)
            def load_lru(n):
                for s in range(CHUNKS):
                    load(n + QB_IN, 0, s, in_v, 0, n * PAIR_N + D)
                for s in range(CHUNKS):
                    load(n + QB_IN, 1, s, in_v, 0, (n * 2) * PART)
                if not isinstance(n, int):
                    sp.wait_ge(gate_ready, n)
                sp.dma_start(gate_raw[:, 0:2, :], ga_v[:, bass.ds(n * 2, 2), :]).then_inc(gate_loaded, 16)
                sp.dma_start(gate_raw[:, 2:4, :], gx_v[:, bass.ds(n * 2, 2), :]).then_inc(gate_loaded, 16)

            load_lru(0)
            with sp.Fori(1, GATE_BLOCKS) as n:
                load_lru(n)
            with sp.Fori(0, Q_WO) as i:
                load_quad(i + QB_OUT, out_v, 0, i * 512)
            load_mlp(QB_MLP1, 1)
            for j in range(PAIRS):
                sp.wait_ge(final_ready, j + 1)
                sp.dma_start(out_l[:, 2 * j:2 * j + 2, :], h[:, 2 * j:2 * j + 2, :]).then_inc(stored, 16)
            sp.wait_ge(stored, 16 * PAIRS)

        @block.gpsimd
        def _(pool):
            nc.gpsimd.memset(ones[:, :], 1.0).then_inc(consts_set, 1)
            nc.gpsimd.memset(eps[:, :], EPS).then_inc(consts_set, 1)
            for buf in (kpad[:, 0], kpad[:, 1]):
                nc.gpsimd.memset(buf.bitcast(F32), 0.0).then_inc(zeros_set, 1)
            nc.gpsimd.memset(vcur[:, :, :, :].bitcast(F32), 0.0).then_inc(zeros_set, 1)
            pool.wait_ge(acc_ready, PAIRS)
            nc.gpsimd.memset(qz[:, :, :, :].bitcast(F32), 0.0).then_inc(zeros_set, 1)
            pool.wait_ge(v_transposed, 1)
            pool.wait_ge(k_ready, 1)
            pool.dma_start(h[:, 0:4, :], x_l[:, 0:4, :]).then_inc(x_again, 16)
            pool.wait_ge(mid_ready, MID_MLP0)
            pool.dma_start(h[:, 4:KT, :], x_l[:, 4:KT, :]).then_inc(x_again_rest, 16)

        @block.scalar
        def _(act):
            def split_hi(q, half_i, s, used=None):
                slot = half_i * CHUNKS + s
                act.wait_ge(raw_loaded[slot], (q + 1) * 16)
                if used is not None:
                    act.wait_ge(wts_used, used)
                elif not (isinstance(q, int) and q == 0 and half_i == 0):
                    act.wait_ge(wts_used, (q * 2 + half_i - 1) * CHUNKS + s + 1)
                nc.scalar.activation(w_hi[:, s, :, :], w_raw[:, slot, :, :], ACT.Copy).then_inc(hi_ready, 1)

            def next_hi(q, half_i, s):
                split_hi(q, 1, s) if half_i == 0 else split_hi(q + 1, 0, s)

            def copy_half(q, half_i, bias=None, done=None):
                act.wait_ge(wts_used, (q * 2 + half_i + 1) * CHUNKS if done is None else done)
                if not (isinstance(q, int) and q == 0 and half_i == 0):
                    act.wait_ge(psum_free, q * 2 + half_i)
                src = ps[:, 2 * half_i:2 * half_i + 2, TOK:2 * TOK]
                if bias is None:
                    nc.scalar.activation(half[:, :, :], src, ACT.Copy).then_inc(half_copied, 1)
                    return
                name, j = bias
                nc.scalar.activation(half[:, 0, :], src[:, 0, :], ACT.Identity, bias=col(name, j * 2))
                nc.scalar.activation(half[:, 1, :], src[:, 1, :], ACT.Identity,
                                     bias=col(name, j * 2 + 1)).then_inc(half_copied, 1)

            def late_hi(q):
                act.wait_ge(raw_loaded[SLOTS - 1], (q + 1) * 16)
                nc.scalar.activation(late_w[0], w_raw[:, SLOTS - 1, :, :], ACT.Copy).then_inc(hi_ready, 1)

            def after_late_hi(q, s):
                split_hi(q + 1, 0, s, q * SLOTS + CHUNKS + s)

            def norm_operand(j, ready, gain):
                act.wait_ge(h_ready, ready)
                act.wait_ge(acc_ready, ready)
                nc.scalar.activation(sq[:, :, :], h_pair(j), ACT.Square).then_inc(sq_ready, 1)
                for b in range(2):
                    last = nc.scalar.activation(xn[:, 0, bass.ds(j * 2 + b, 1), :], h[:, bass.ds(j * 2 + b, 1), :],
                                                ACT.Copy, scale=col(gain, j * 2 + b))
                last.then_inc(xn_hi, 1)

            def root(n):
                act.wait_ge(stats_done, n + 1)
                nc.scalar.activation(rms[:, :], x3[:, 0:TOK], ACT.Sqrt, bias=eps[:, :], scale=1.0 / D
                                     ).then_inc(rms_ready, 1)

            def residual(q, half_i, j, bias=None, norm=None, done=None):
                copy_half(q, half_i, bias, done)
                if norm is not None:
                    n, gain = norm
                    norm_operand(j, j + (8 * (n - 1) + 1), gain)

            def late_residuals(q, bias, norm):
                copy_half(q, 0, (bias, 0), late_done(q))
                after_late_hi(q, 3)
                n, gain = norm
                norm_operand(0, 8 * (n - 1) + 1, gain)
                residual(q, 1, 1, (bias, 1), norm)

            act.wait_ge(consts_set, 2)
            nc.scalar.activation(rms[:, 0:1], eps[:, :], ACT.Sqrt)
            for s in range(CHUNKS):
                split_hi(0, 0, s)
                if s == 0:
                    act.wait_ge(gain_loaded, 16)
                act.wait_ge(x_loaded[s], 16)
                for kt in range(4 * s, 4 * s + 4):
                    last = nc.scalar.activation(xn[:, 0, kt, :], h[:, kt, :], ACT.Copy, scale=col("mix0", kt))
                    if kt % 2:
                        last.then_inc(xn_hi, 1)

            def first_squares(pairs):
                for j in pairs:
                    nc.scalar.activation(first_sq[:, 2 * j:2 * j + 2, :], h_pair(j), ACT.Square
                                         ).then_inc(sq_ready, 1)

            def roped_hi(j):
                act.wait_ge(roped, j + 2)
                nc.scalar.activation(qz[:, 0, :, :].rearrange("p b (c t) -> p b c t", c=3)[:, :, 0:3:2, :],
                                     qa[:, :, :].rearrange("p b (t c x) -> p (b t) c x", t=2, c=2),
                                     ACT.Copy).then_inc(q_hi, 1)

            def pt_split_hi(j):
                act.wait_ge(transposed, j + 1)
                nc.scalar.activation(pt[:, 0, :, :], xs, ACT.Copy).then_inc(pt_hi, 1)

            def softmax_exp(j, b):
                act.wait_ge(max_ready, j + 1)
                if b == 0:
                    nc.scalar.activation(s_esink, s_sink, ACT.Exp)
                for m in range(4 * b, 4 * b + 4):
                    last = nc.scalar.activation(prob[:, m * PART:(m + 1) * PART],
                                                xs[:, b, (m % 4) * PART:(m % 4 + 1) * PART], ACT.Exp,
                                                bias=s_neg[:, m:m + 1], scale=SCALE, accum_out=s_sum[:, m:m + 1])
                last.then_inc(exp_done, 1)

            def att_hi(j):
                act.wait_ge(att_done, j + 1)
                nc.scalar.activation(mid[:, 0, bass.ds(j * 2, 2), :], x0.rearrange("p (b t) -> p b t", b=2),
                                     ACT.Copy).then_inc(att_out_hi, 1)

            def qkv_bias(n, tile, out_a, out_b, ready):
                act.wait_ge(qkv_scaled, n + 1)
                nc.scalar.activation(out_a, u[:, 0, :], ACT.Identity, bias=col("b_qkv", tile))
                nc.scalar.activation(out_b, u[:, 1, :], ACT.Identity, bias=col("b_qkv", tile + 1)
                                     ).then_inc(ready, 1)

            def q_bias(j):
                qkv_bias(j + 2, j * 2, u[:, 0, :], u[:, 1, :], rope_in)

            def vcur_split_hi(g):
                nc.scalar.activation(vcur[:, 0, :, HD:2 * HD], vraw[:, g, :, :], ACT.Copy).then_inc(vcur_hi, 1)

            for s, squares in enumerate(((0, 1, 2), (3, 4, 5), (6, 7))):
                next_hi(0, 0, s)
                first_squares(squares)
            copy_half(0, 0)
            next_hi(0, 0, 3)
            next_hi(0, 1, 0)
            next_hi(0, 1, 1)
            next_hi(0, 1, 2)
            root(0)
            copy_half(0, 1)
            next_hi(0, 1, 3)
            act.wait_ge(vec_loaded, 16)
            qkv_bias(0, 16, u[:, 0, :], u[:, 1, :], rope_in)
            next_hi(1, 0, 0)
            act.wait_ge(roped, 1)
            nc.scalar.activation(kswap[HD:PART, :, :], qa[0:HD, :, :], ACT.Copy)
            nc.scalar.activation(kswap[0:HD, :, :], qa[HD:PART, :, :], ACT.Copy).then_inc(kswapped, 1)
            qkv_bias(1, 18, vt[:, 0, HD:HD + TOK], vt[:, 1, HD:HD + TOK], vt_ready)
            act.wait_ge(zeros_set, 4)
            act.wait_ge(kswapped, 1)
            kv = kpad[:, 0, :, :, HD:HD + TOK].rearrange("p (b s) a t -> p b s a t", s=2)
            for part, side, src in ((0, 0, qa), (0, 1, kswap), (1, 1, qa), (1, 0, kswap)):
                r = slice(HD * part, HD * part + HD)
                last = nc.scalar.activation(kv[r, :, side, part, :], src[r, :, :], ACT.Copy)
            last.then_inc(k_hi, 1)
            for s in range(1, 3):
                next_hi(1, 0, s)
            copy_half(1, 0)
            next_hi(1, 0, 3)
            q_bias(0)
            next_hi(1, 1, 0)
            roped_hi(0)
            next_hi(1, 1, 1)
            next_hi(1, 1, 2)
            softmax_exp(0, 0)
            softmax_exp(0, 1)
            copy_half(1, 1)
            q_bias(1)
            next_hi(1, 1, 3)

            def attention_step(q, half_i, j):
                next_hi(q, half_i, 0)
                pt_split_hi(j - 1)
                roped_hi(j)
                if half_i == 0:
                    act.wait_ge(v_read, 1)
                    vcur_split_hi(q - 2)
                next_hi(q, half_i, 1)
                next_hi(q, half_i, 2)
                softmax_exp(j, 0)
                softmax_exp(j, 1)
                copy_half(q, half_i)
                att_hi(j - 1)
                q_bias(j + 1)
                next_hi(q, half_i, 3)

            with act.Fori(2, Q_QKV) as q:
                attention_step(q, 0, q * 2 - 3)
                attention_step(q, 1, q * 2 - 2)

            last = PAIRS - 1
            next_hi(QB_WO, 0, 0)
            roped_hi(last)
            pt_split_hi(last - 1)
            vcur_split_hi(KV_HEADS - 1)
            next_hi(QB_WO, 0, 1)
            next_hi(QB_WO, 0, 2)
            softmax_exp(last, 0)
            softmax_exp(last, 1)
            att_hi(last - 1)
            late_hi(QB_WO)
            after_late_hi(QB_WO, 0)
            pt_split_hi(last)
            after_late_hi(QB_WO, 1)
            att_hi(last)
            after_late_hi(QB_WO, 2)
            late_residuals(QB_WO, "b_o", (1, "mlp0"))

            def residual_step(q, half_i, j, bias=None, norm=None):
                for s in range(3):
                    next_hi(q, half_i, s)
                residual(q, half_i, j, bias, norm)
                next_hi(q, half_i, 3)

            with act.Fori(1, Q_WO) as i:
                residual_step(i + QB_WO, 0, i * 2, ("b_o", i * 2), (1, "mlp0"))
                residual_step(i + QB_WO, 1, i * 2 + 1, ("b_o", i * 2 + 1), (1, "mlp0"))

            def up_step(q, half_i, j, relus, norm=None):
                for s in range(3):
                    next_hi(q, half_i, s)
                if norm is not None:
                    root(norm)
                copy_half(q, half_i)
                act.wait_ge(relu_ready, relus + 1)
                nc.scalar.activation(mid[:, 0, bass.ds(j * 2, 2), :], u[:, :, :], ACT.Square).then_inc(mid_hi, 1)
                next_hi(q, half_i, 3)

            def mlp(base, norm, gain, relus):
                def up_quad(q, i, r, norm=None):
                    up_step(q, 0, i * 2, r, norm)
                    up_step(q, 1, i * 2 + 1, r + 1)

                up_quad(base, 0, relus, norm)
                with act.Fori(1, 4) as i:
                    up_quad(i + base, i, i * 2 + relus)
                with act.Fori(0, 4) as i:
                    residual_step(i + (base + 4), 0, i * 2)
                    residual_step(i + (base + 4), 1, i * 2 + 1)
                with act.Fori(1, GROUPS - 1) as g:
                    with act.Fori(0, 4) as i:
                        up_quad(g * 8 + i + base, i, g * 8 + i * 2 + relus)
                    with act.Fori(0, 4) as i:
                        residual_step(g * 8 + i + (base + 4), 0, i * 2)
                        residual_step(g * 8 + i + (base + 4), 1, i * 2 + 1)
                last = base + 8 * (GROUPS - 1)
                with act.Fori(0, 4) as i:
                    up_quad(i + last, i, i * 2 + (8 * (GROUPS - 1) + relus))
                return last + 4

            last = mlp(QB_MLP0, 1, "mlp0", 0)
            with act.Fori(0, 4) as i:
                residual_step(i + last, 0, i * 2, None, (2, "mix1"))
                residual_step(i + last, 1, i * 2 + 1, None, (2, "mix1"))

            def gate_sigmoids(n):
                act.wait_ge(gates_done, n + 1)
                for b in range(2):
                    nc.scalar.activation(g_r[:, b, :], aux[:, 0, b * TOK:(b + 1) * TOK], ACT.Sigmoid,
                                         bias=col("ga_b", n * 2 + b))
                for b in range(2):
                    last = nc.scalar.activation(g_i[:, b, :], aux[:, 1, b * TOK:(b + 1) * TOK], ACT.Sigmoid,
                                                bias=col("gx_b", n * 2 + b))
                last.then_inc(sig_done, 1)

            def decay_tanh(n):
                act.wait_ge(sig_done, n + 1)
                for b in range(2):
                    nc.scalar.activation(th[:, b, :], g_r[:, b, :], ACT.Tanh,
                                         scale=lru[:, 1, bass.ds(n * 2 + b, 1)])

            def decay_exp(n):
                for b in range(2):
                    last = nc.scalar.activation(a_exp[:, b, :], g_r[:, b, :], ACT.Exp,
                                                scale=lru[:, 0, bass.ds(n * 2 + b, 1)])
                last.then_inc(decay_in, 1)

            def y_bias_and_square(n):
                act.wait_ge(y_scaled, n + 1)
                if not (isinstance(n, int) and n == 0):
                    act.wait_ge(gelu_ready, n)
                for b in range(2):
                    last = nc.scalar.activation(y[:, b, :], u[:, b, :], ACT.Identity, bias=col("b_in", n * 2 + b))
                last.then_inc(y_ready, 1)
                act.wait_ge(y_ready, n + 1)
                nc.scalar.activation(ys[:, :, :], y[:, :, :], ACT.Square, scale=0.044715 ** 0.5).then_inc(y_sq, 1)

            def y_tanh_step(n):
                act.wait_ge(z_ready, n + 1)
                nc.scalar.activation(ys[:, :, :], ys[:, :, :], ACT.Tanh, scale=0.7978845608028654).then_inc(y_tanh, 1)

            def roots(n):
                act.wait_ge(decay_in, n + 1)
                nc.scalar.activation(root_t[:, :, :], th[:, :, :], ACT.Sqrt).then_inc(root_done, 1)

            def lru_split_hi(n):
                act.wait_ge(lru_out, n + 1)
                nc.scalar.activation(mid[:, 0, bass.ds(n * 2, 2), :], v[:, :, :], ACT.Copy).then_inc(lru_hi, 1)

            def gate_split_hi(n):
                act.wait_ge(gate_loaded, (n + 1) * 32)
                if not (isinstance(n, int) and n == 0):
                    act.wait_ge(gates_done, n)
                nc.scalar.activation(gate_hi[:, :, :], gate_raw[:, :, :], ACT.Copy).then_inc(gate_hi_ready, 1)

            def conv_first_tap(n):
                act.wait_ge(x_scaled, n + 1)
                for b in range(2):
                    last = nc.scalar.activation(xb[:, b, TAPS - 1:], u[:, b, :], ACT.Identity,
                                                bias=col("b_in", n * 2 + (KT + b)))
                last.then_inc(xb_ready, 1)
                act.wait_ge(xb_ready, n + 1)
                for b in range(2):
                    last = nc.scalar.activation(xc[:, b, :], xb[:, b, 0:TOK], ACT.Identity,
                                                bias=col("conv_b", n * 2 + b), scale=col("conv_w", n * 2 + b))
                last.then_inc(tap_ready, 1)

            def xc_split_hi(n):
                act.wait_ge(xc_ready, n + 1)
                nc.scalar.activation(xc_split[:, 0, :, :], xc[:, :, :], ACT.Copy).then_inc(xc_hi, 1)

            def lru_quad(q, n, before, recur):
                if before:
                    y_bias_and_square(n - 1)
                next_hi(q, 0, 0)
                if before:
                    gate_sigmoids(n - 1)
                    y_tanh_step(n - 1)
                if before:
                    decay_tanh(n - 1)
                if recur:
                    lru_split_hi(n - 2)
                next_hi(q, 0, 1)
                if before:
                    decay_exp(n - 1)
                next_hi(q, 0, 2)
                if isinstance(n, int) and n == 0:
                    act.wait_ge(lam_abs, 1)
                    nc.scalar.activation(lru[:, 3, :], lru[:, 2, :], ACT.Exp, scale=-1.0).then_inc(lam_exp, 1)
                    root(2)
                copy_half(q, 0)
                next_hi(q, 0, 3)
                gate_split_hi(n)
                conv_first_tap(n)
                next_hi(q, 1, 0)
                if before:
                    roots(n - 1)
                next_hi(q, 1, 1)
                xc_split_hi(n)
                next_hi(q, 1, 2)
                copy_half(q, 1)
                next_hi(q, 1, 3)

            lru_quad(QB_IN, 0, False, False)
            lru_quad(QB_IN + 1, 1, True, False)
            with act.Fori(2, GATE_BLOCKS) as n:
                lru_quad(n + QB_IN, n, True, True)
            q, n = QB_OUT, GATE_BLOCKS - 1
            y_bias_and_square(n)
            next_hi(q, 0, 0)
            gate_sigmoids(n)
            y_tanh_step(n)
            decay_tanh(n)
            lru_split_hi(n - 1)
            next_hi(q, 0, 1)
            next_hi(q, 0, 2)
            decay_exp(n)
            roots(n)
            late_hi(q)
            after_late_hi(q, 0)
            lru_split_hi(n)
            after_late_hi(q, 1)
            after_late_hi(q, 2)
            late_residuals(q, "b_out", (3, "mlp1"))
            with act.Fori(1, Q_WO) as i:
                residual_step(i + QB_OUT, 0, i * 2, ("b_out", i * 2), (3, "mlp1"))
                residual_step(i + QB_OUT, 1, i * 2 + 1, ("b_out", i * 2 + 1), (3, "mlp1"))

            last = mlp(QB_MLP1, 3, "mlp1", GROUPS * PAIRS)

            def final_step(q, half_i, j, more=True):
                if more:
                    for s in range(3):
                        next_hi(q, half_i, s)
                copy_half(q, half_i)
                act.wait_ge(h_ready, j + 25)
                act.wait_ge(acc_ready, j + 32)
                nc.scalar.activation(sq[:, :, :], h_pair(j), ACT.Square).then_inc(sq_ready, 1)
                act.wait_ge(sq_ready, j + 33)
                for b in range(2):
                    one = h[:, bass.ds(j * 2 + b, 1), :]
                    done = nc.scalar.activation(one, one, ACT.Copy, scale=col("fin", j * 2 + b))
                done.then_inc(hg_ready, 1)
                if more:
                    next_hi(q, half_i, 3)

            with act.Fori(0, 3) as i:
                final_step(i + last, 0, i * 2)
                final_step(i + last, 1, i * 2 + 1)
            final_step(last + 3, 0, 6)
            nc.scalar.activation(rms[:, 0:1], eps[:, :], ACT.Sqrt)
            final_step(last + 3, 1, 7, False)
            root(4)

        @block.vector
        def _(dve):
            step = Count(dve_step)

            def then(ins):
                step.up(ins)
                dve.wait_ge(dve_step, step.value)

            def split_lo(q, half_i, s):
                slot = half_i * CHUNKS + s
                dve.wait_ge(hi_ready, (q * 2 + half_i) * CHUNKS + s + 1)
                nc.vector.tensor_tensor(w_lo[:, s, :, :], w_raw[:, slot, :, :], w_hi[:, s, :, :].bitcast(F32),
                                        ALU.subtract).then_inc(lo_ready, 1)

            def late_lo(q):
                dve.wait_ge(hi_ready, (q + 1) * SLOTS)
                nc.vector.tensor_tensor(late_w[1], w_raw[:, SLOTS - 1, :, :], late_w[0].bitcast(F32), ALU.subtract
                                        ).then_inc(lo_ready, 1)

            def next_lo(q, half_i, s):
                split_lo(q, 1, s) if half_i == 0 else split_lo(q + 1, 0, s)

            def add_halves(q, half_i):
                dve.wait_ge(half_copied, q * 2 + half_i + 1)
                nc.vector.tensor_tensor(u[:, :, :], ps[:, 2 * half_i:2 * half_i + 2, 0:TOK], half[:, :, :],
                                        ALU.add).then_inc(psum_free, 1)
                dve.wait_ge(psum_free, q * 2 + half_i + 1)

            def sum_squares():
                return nc.vector.tensor_tensor(acc[:, :, :], acc[:, :, :], sq[:, :, :], ALU.add)

            def inverse_root(n):
                dve.wait_ge(rms_ready, n + 1)
                then(nc.vector.reciprocal(rstd[:, :], rms[:, :]))
                then(nc.vector.memset(acc[:, :, :], 0.0))

            def norm_operand(j, ready, gain):
                dve.wait_ge(xn_hi, ready + 8)
                for b in range(2):
                    last = nc.vector.scalar_tensor_tensor(
                        xn[:, 1, bass.ds(j * 2 + b, 1), :], in0=h[:, bass.ds(j * 2 + b, 1), :],
                        scalar=col(gain, j * 2 + b), in1=xn[:, 0, bass.ds(j * 2 + b, 1), :].bitcast(F32),
                        op0=ALU.mult, op1=ALU.subtract)
                last.then_inc(xn_ready, 1)
                dve.wait_ge(sq_ready, ready + 8)
                sum_squares().then_inc(acc_ready, 1)

            def residual(q, half_i, j, norm=None):
                add_halves(q, half_i)
                add = nc.vector.tensor_tensor(h_pair(j), h_pair(j), u[:, :, :], ALU.add)
                if norm is not None:
                    n, gain = norm
                    add.then_inc(h_ready, 1)
                    norm_operand(j, j + (8 * (n - 1) + 1), gain)

            def residual_step(q, half_i, j, norm=None):
                for s in range(3):
                    next_lo(q, half_i, s)
                residual(q, half_i, j, norm)
                next_lo(q, half_i, 3)

            def late_residuals(q, norm):
                add_halves(q, 0)
                nc.vector.tensor_tensor(h_pair(0), h_pair(0), u[:, :, :], ALU.add).then_inc(h_ready, 1)
                next_lo(q, 1, 3)
                n, gain = norm
                norm_operand(0, 8 * (n - 1) + 1, gain)
                residual(q, 1, 1, norm)

            then(nc.vector.memset(acc[:, :, :], 0.0))
            dve.wait_ge(gain_loaded, 16)
            for s in range(CHUNKS):
                split_lo(0, 0, s)
                for kt in range(4 * s, 4 * s + 4):
                    if kt % 2 == 0:
                        dve.wait_ge(xn_hi, kt // 2 + 1)
                    last = nc.vector.scalar_tensor_tensor(xn[:, 1, kt, :], in0=h[:, kt, :], scalar=col("mix0", kt),
                                                          in1=xn[:, 0, kt, :].bitcast(F32),
                                                          op0=ALU.mult, op1=ALU.subtract)
                    if kt % 2:
                        last.then_inc(xn_ready, 1)

            def sum_first_squares(pairs):
                for j in pairs:
                    dve.wait_ge(sq_ready, j + 1)
                    if j:
                        dve.wait_ge(acc_ready, j)
                    nc.vector.tensor_tensor(acc[:, :, :], acc[:, :, :], first_sq[:, 2 * j:2 * j + 2, :],
                                            ALU.add).then_inc(acc_ready, 1)

            def qkv_scale(q, half_i, added=False):
                if not added:
                    add_halves(q, half_i)
                nc.vector.tensor_tensor(u[:, :, :], u[:, :, :], bc2(rstd[:, :]), ALU.mult).then_inc(qkv_scaled, 1)

            def rope_cos(n):
                dve.wait_ge(rope_in, n + 1)
                nc.vector.tensor_tensor(qa, u[:, :, :], bc2(cos), ALU.mult).then_inc(cos_done, 1)

            def rope(n):
                dve.wait_ge(rotated, n + 1)
                nc.vector.tensor_tensor(qb, x3.rearrange("p (b t) -> p b t", b=2), bc2(sin), ALU.mult
                                        ).then_inc(rot_read, 1)
                dve.wait_ge(cos_done, n + 1)
                dve.wait_ge(rot_read, n + 1)
                nc.vector.tensor_tensor(qa, qa, qb, ALU.add).then_inc(roped, 1)

            def q_split_lo(j):
                dve.wait_ge(q_hi, j + 1)
                qc = qz[:, :, :, :].rearrange("p h b (c t) -> p h b c t", c=3)
                nc.vector.tensor_tensor(qc[:, 1, :, 0:3:2, :],
                                        qa[:, :, :].rearrange("p b (t c x) -> p (b t) c x", t=2, c=2),
                                        qc[:, 0, :, 0:3:2, :].bitcast(F32), ALU.subtract).then_inc(q_ready, 1)

            def softmax_max(j):
                dve.wait_ge(scored, j + 1)
                first = xs.rearrange("p b (t a c x) -> p b t a c x", t=2, a=2, c=2)
                then(nc.vector.memset(first[0:HD, :, 0, :, 0, :], NEG_BIG))
                then(nc.vector.reduce_max(s_max, xs.rearrange("p b (m k) -> p (b m) k", k=PART), AX_X))
                then(nc.vector.scalar_tensor_tensor(s_neg, in0=s_max, scalar=-SCALE,
                                                    in1=neg_sinks[:, bass.ds(j * 8, 8)], op0=ALU.mult, op1=ALU.min))
                nc.vector.tensor_tensor(s_sink, vec[:, bass.ds(VEC["sinks"] + j * 8, 8)], s_neg, ALU.add
                                        ).then_inc(max_ready, 1)

            def softmax_scale(j):
                dve.wait_ge(exp_done, j * 2 + 2)
                p8 = prob.rearrange("p (m k) -> p m k", k=PART)
                then(nc.vector.tensor_tensor(s_den, s_sum, s_esink, ALU.add))
                then(nc.vector.reciprocal(s_rden, s_den))
                nc.vector.tensor_tensor(p8, p8, s_rden.unsqueeze(2).to_broadcast([PART, 8, PART]), ALU.mult
                                        ).then_inc(probs_ready, 1)

            def pt_split_lo(j):
                dve.wait_ge(pt_hi, j + 1)
                nc.vector.tensor_tensor(pt[:, 1, :, :], xs, pt[:, 0, :, :].bitcast(F32), ALU.subtract
                                        ).then_inc(pt_ready, 1)

            def att_lo(j):
                dve.wait_ge(att_out_hi, j + 1)
                nc.vector.tensor_tensor(mid[:, 1, bass.ds(j * 2, 2), :], x0.rearrange("p (b t) -> p b t", b=2),
                                        mid[:, 0, bass.ds(j * 2, 2), :].bitcast(F32), ALU.subtract
                                        ).then_inc(mid_ready, 1)

            def vcur_split_lo(g):
                dve.wait_ge(vcur_hi, g + 1)
                nc.vector.tensor_tensor(vcur[:, 1, :, HD:2 * HD], vraw[:, g, :, :],
                                        vcur[:, 0, :, HD:2 * HD].bitcast(F32), ALU.subtract
                                        ).then_inc(vcur_ready, 1)

            for s, squares in enumerate(((0, 1, 2), (3, 4, 5), (6, 7))):
                next_lo(0, 0, s)
                sum_first_squares(squares)
            next_lo(0, 0, 3)
            add_halves(0, 0)
            for s in range(3):
                next_lo(0, 1, s)
            dve.wait_ge(rms_ready, 1)
            then(nc.vector.reciprocal(rstd[:, :], rms[:, :]))
            qkv_scale(0, 0, added=True)
            next_lo(0, 1, 3)
            dve.wait_ge(const_loaded, 16)
            rope_cos(0)
            rope(0)
            then(nc.vector.memset(vt[:, :, 0:HD], 0.0))
            qkv_scale(0, 1)
            next_lo(1, 0, 0)
            dve.wait_ge(k_hi, 1)
            kv = kpad[:, :, :, :, HD:HD + TOK].rearrange("p h (b s) a t -> p h b s a t", s=2)
            for part, side, src in ((0, 0, qa), (0, 1, kswap), (1, 1, qa), (1, 0, kswap)):
                r = slice(HD * part, HD * part + HD)
                last = nc.vector.tensor_tensor(kv[r, 1, :, side, part, :], src[r, :, :],
                                               kv[r, 0, :, side, part, :].bitcast(F32), ALU.subtract)
            last.then_inc(k_ready, 1)
            next_lo(1, 0, 1)
            next_lo(1, 0, 2)
            qkv_scale(1, 0)
            dve.wait_ge(v_transposed, 1)
            for b in range(2):
                last = nc.vector.tensor_copy(vraw[:, 2 * b:2 * b + 2, :, :],
                                             xs[:, b, :].rearrange("p (c k d) -> p k c d", c=4, k=2))
            last.then_inc(v_read, 1)
            next_lo(1, 0, 3)
            rope_cos(1)
            rope(1)
            dve.wait_ge(vec_loaded, 16)
            then(nc.vector.tensor_scalar(neg_sinks, vec[:, VEC["sinks"]:VEC["sinks"] + 64], -1.0, None, ALU.mult))
            q_split_lo(0)
            then(nc.vector.memset(acc[:, :, :], 0.0))
            next_lo(1, 1, 0)
            next_lo(1, 1, 1)
            next_lo(1, 1, 2)
            softmax_max(0)
            qkv_scale(1, 1)
            softmax_scale(0)
            next_lo(1, 1, 3)

            def attention_step(q, half_i, j):
                rope_cos(j + 1)
                rope(j + 1)
                pt_split_lo(j - 1)
                q_split_lo(j)
                if half_i == 0:
                    vcur_split_lo(q - 2)
                next_lo(q, half_i, 0)
                next_lo(q, half_i, 1)
                softmax_max(j)
                next_lo(q, half_i, 2)
                qkv_scale(q, half_i)
                att_lo(j - 1)
                softmax_scale(j)
                next_lo(q, half_i, 3)

            with repeat(dve, 2, Q_QKV, step, 10) as q:
                attention_step(q, 0, q * 2 - 3)
                attention_step(q, 1, q * 2 - 2)

            last = PAIRS - 1
            rope_cos(last + 1)
            rope(last + 1)
            next_lo(QB_WO, 0, 0)
            q_split_lo(last)
            pt_split_lo(last - 1)
            vcur_split_lo(KV_HEADS - 1)
            next_lo(QB_WO, 0, 1)
            next_lo(QB_WO, 0, 2)
            softmax_max(last)
            softmax_scale(last)
            att_lo(last - 1)
            late_lo(QB_WO)
            next_lo(QB_WO, 1, 0)
            pt_split_lo(last)
            next_lo(QB_WO, 1, 1)
            att_lo(last)
            next_lo(QB_WO, 1, 2)
            dve.wait_ge(x_again, 16)
            late_residuals(QB_WO, (1, "mlp0"))
            dve.wait_ge(x_again_rest, 16)
            with dve.Fori(1, Q_WO) as i:
                residual_step(i + QB_WO, 0, i * 2, (1, "mlp0"))
                residual_step(i + QB_WO, 1, i * 2 + 1, (1, "mlp0"))

            def up_step(q, half_i, j, relus, norm=None):
                for s in range(3):
                    next_lo(q, half_i, s)
                if norm is not None:
                    inverse_root(norm)
                add_halves(q, half_i)
                nc.vector.scalar_tensor_tensor(u[:, :, :], in0=u[:, :, :], scalar=0.0, in1=bc2(rstd[:, :]),
                                               op0=ALU.max, op1=ALU.mult).then_inc(relu_ready, 1)
                dve.wait_ge(relu_ready, relus + 1)
                nc.vector.tensor_tensor(v[:, :, :], u[:, :, :], u[:, :, :], ALU.mult).then_inc(squared, 1)
                dve.wait_ge(squared, relus + 1)
                dve.wait_ge(mid_hi, relus + 1)
                nc.vector.tensor_tensor(mid[:, 1, bass.ds(j * 2, 2), :], v[:, :, :],
                                        mid[:, 0, bass.ds(j * 2, 2), :].bitcast(F32), ALU.subtract
                                        ).then_inc(mid_ready, 1)
                next_lo(q, half_i, 3)

            def mlp(base, norm, gain, relus):
                def up_quad(q, i, r, norm=None):
                    up_step(q, 0, i * 2, r, norm)
                    up_step(q, 1, i * 2 + 1, r + 1)

                up_quad(base, 0, relus, norm)
                with dve.Fori(1, 4) as i:
                    up_quad(i + base, i, i * 2 + relus)
                with dve.Fori(0, 4) as i:
                    residual_step(i + (base + 4), 0, i * 2)
                    residual_step(i + (base + 4), 1, i * 2 + 1)
                with dve.Fori(1, GROUPS - 1) as g:
                    with dve.Fori(0, 4) as i:
                        up_quad(g * 8 + i + base, i, g * 8 + i * 2 + relus)
                    with dve.Fori(0, 4) as i:
                        residual_step(g * 8 + i + (base + 4), 0, i * 2)
                        residual_step(g * 8 + i + (base + 4), 1, i * 2 + 1)
                last = base + 8 * (GROUPS - 1)
                with dve.Fori(0, 4) as i:
                    up_quad(i + last, i, i * 2 + (8 * (GROUPS - 1) + relus))
                return last + 4

            last = mlp(QB_MLP0, 1, "mlp0", 0)
            with dve.Fori(0, 4) as i:
                residual_step(i + last, 0, i * 2, (2, "mix1"))
                residual_step(i + last, 1, i * 2 + 1, (2, "mix1"))

            def softplus_of_minus_lambda():
                lam = vec[:, VEC["lam"]:VEC["lam"] + KT]
                r = [lru[:, i, :] for i in range(12)]
                then(nc.vector.tensor_scalar(r[4], lam, -1.0, None, ALU.mult))
                nc.vector.tensor_tensor(r[2], lam, r[4], ALU.max).then_inc(lam_abs, 1)
                dve.wait_ge(lam_exp, 1)
                then(nc.vector.tensor_scalar(r[5], r[3], 2.0, None, ALU.add))
                then(nc.vector.reciprocal(r[6], r[5]))
                then(nc.vector.tensor_tensor(r[7], r[3], r[6], ALU.mult))
                then(nc.vector.tensor_tensor(r[8], r[7], r[7], ALU.mult))
                then(nc.vector.tensor_scalar(r[9], r[8], 1.0 / 17, None, ALU.mult))
                for k in (15, 13, 11, 9, 7, 5, 3):
                    then(nc.vector.scalar_tensor_tensor(r[9], in0=r[9], scalar=1.0 / k, in1=r[8],
                                                        op0=ALU.add, op1=ALU.mult))
                then(nc.vector.scalar_tensor_tensor(r[10], in0=r[9], scalar=1.0, in1=r[7],
                                                    op0=ALU.add, op1=ALU.mult))
                then(nc.vector.tensor_scalar(r[11], r[4], 0.0, 0.5, ALU.max, ALU.mult))
                then(nc.vector.tensor_tensor(r[11], r[11], r[10], ALU.add))
                nc.vector.tensor_scalar(lru[:, 0, :], r[11], -16.0, None, ALU.mult)
                then(nc.vector.tensor_scalar(lru[:, 1, :], r[11], 8.0, None, ALU.mult))

            def gate_input(n):
                dve.wait_ge(sig_done, n + 1)
                then(nc.vector.tensor_tensor(driven[:, :, :], g_i[:, :, :], xc[:, :, :], ALU.mult))

            def decay_terms(n):
                dve.wait_ge(decay_in, n + 1)
                then(nc.vector.scalar_tensor_tensor(decay[:, :, :], in0=a_exp[:, :, :], scalar=1.0,
                                                    in1=th[:, :, :], op0=ALU.add, op1=ALU.mult))
                then(nc.vector.tensor_scalar(decay[:, :, :], decay[:, :, :], -1.0, 1.0, ALU.mult, ALU.add))

            def recurrence(n):
                dve.wait_ge(root_done, n + 1)
                then(nc.vector.scalar_tensor_tensor(a_exp[:, :, :], in0=a_exp[:, :, :], scalar=1.0,
                                                    in1=root_t[:, :, :], op0=ALU.add, op1=ALU.mult))
                then(nc.vector.tensor_tensor(driven[:, :, :], driven[:, :, :], a_exp[:, :, :], ALU.mult))
                for b in range(2):
                    ins = nc.vector.tensor_tensor_scan(v[:, b, :], decay[:, b, :], driven[:, b, :], 0.0,
                                                       ALU.mult, ALU.add)
                ins.then_inc(scanned, 1)

            def recurrent_output(n):
                dve.wait_ge(scanned, n + 1)
                nc.vector.scalar_tensor_tensor(v[:, :, :], in0=v[:, :, :], scalar=0.5, in1=gelu[:, :, :],
                                               op0=ALU.mult, op1=ALU.mult).then_inc(lru_out, 1)

            def gelu_argument(n):
                dve.wait_ge(y_sq, n + 1)
                nc.vector.scalar_tensor_tensor(ys[:, :, :], in0=ys[:, :, :], scalar=1.0, in1=y[:, :, :],
                                               op0=ALU.add, op1=ALU.mult).then_inc(z_ready, 1)

            def gelu_product(n, outs):
                dve.wait_ge(y_tanh, n + 1)
                if outs is not None:
                    dve.wait_ge(lru_out, outs)
                nc.vector.scalar_tensor_tensor(gelu[:, :, :], in0=ys[:, :, :], scalar=1.0, in1=y[:, :, :],
                                               op0=ALU.add, op1=ALU.mult).then_inc(gelu_ready, 1)

            def lru_split_lo(n):
                dve.wait_ge(lru_hi, n + 1)
                nc.vector.tensor_tensor(mid[:, 1, bass.ds(n * 2, 2), :], v[:, :, :],
                                        mid[:, 0, bass.ds(n * 2, 2), :].bitcast(F32), ALU.subtract
                                        ).then_inc(mid_ready, 1)

            def gate_split_lo(n):
                dve.wait_ge(gate_hi_ready, n + 1)
                nc.vector.tensor_tensor(gate_lo[:, :, :], gate_raw[:, :, :], gate_hi[:, :, :].bitcast(F32),
                                        ALU.subtract).then_inc(gate_ready, 1)

            def scaled(q, half_i):
                add_halves(q, half_i)
                return nc.vector.tensor_tensor(u[:, :, :], u[:, :, :], bc2(rstd[:, :]), ALU.mult)

            def conv(n):
                dve.wait_ge(tap_ready, n + 1)
                for tap in range(1, TAPS):
                    for b in range(2):
                        last = nc.vector.scalar_tensor_tensor(
                            xc[:, b, :], in0=xb[:, b, tap:tap + TOK], scalar=col("conv_w", n * 2 + (b + tap * KT)),
                            in1=xc[:, b, :], op0=ALU.mult, op1=ALU.add)
                    if tap < TAPS - 1:
                        then(last)
                last.then_inc(xc_ready, 1)

            def xc_split_lo(n):
                dve.wait_ge(xc_hi, n + 1)
                nc.vector.tensor_tensor(xc_split[:, 1, :, :], xc[:, :, :], xc_split[:, 0, :, :].bitcast(F32),
                                        ALU.subtract).then_inc(xc_lo, 1)

            def lru_quad(q, n, before, recur):
                if before:
                    gelu_argument(n - 1)
                next_lo(q, 0, 0)
                if recur:
                    recurrence(n - 2)
                    recurrent_output(n - 2)
                if before:
                    gate_input(n - 1)
                if before:
                    gelu_product(n - 1, n - 1 if recur else None)
                next_lo(q, 0, 1)
                if recur:
                    lru_split_lo(n - 2)
                if before:
                    decay_terms(n - 1)
                next_lo(q, 0, 2)
                if isinstance(n, int) and n == 0:
                    softplus_of_minus_lambda()
                    then(nc.vector.memset(xb[:, :, 0:TAPS - 1], 0.0))
                    inverse_root(2)
                scaled(q, 0).then_inc(x_scaled, 1)
                next_lo(q, 0, 3)
                gate_split_lo(n)
                conv(n)
                next_lo(q, 1, 0)
                xc_split_lo(n)
                next_lo(q, 1, 1)
                next_lo(q, 1, 2)
                scaled(q, 1).then_inc(y_scaled, 1)
                next_lo(q, 1, 3)

            lru_quad(QB_IN, 0, False, False)
            lru_quad(QB_IN + 1, 1, True, False)
            with repeat(dve, 2, GATE_BLOCKS, step, 7) as n:
                lru_quad(n + QB_IN, n, True, True)
            q, n = QB_OUT, GATE_BLOCKS - 1
            gelu_argument(n)
            next_lo(q, 0, 0)
            recurrence(n - 1)
            recurrent_output(n - 1)
            gate_input(n)
            gelu_product(n, n)
            next_lo(q, 0, 1)
            lru_split_lo(n - 1)
            next_lo(q, 0, 2)
            decay_terms(n)
            recurrence(n)
            recurrent_output(n)
            lru_split_lo(n)
            late_lo(q)
            for s in range(3):
                next_lo(q, 1, s)
            late_residuals(q, (3, "mlp1"))
            with dve.Fori(1, Q_WO) as i:
                residual_step(i + QB_OUT, 0, i * 2, (3, "mlp1"))
                residual_step(i + QB_OUT, 1, i * 2 + 1, (3, "mlp1"))

            last = mlp(QB_MLP1, 3, "mlp1", GROUPS * PAIRS)

            def final_step(q, half_i, j, more=True):
                if more:
                    for s in range(3):
                        next_lo(q, half_i, s)
                add_halves(q, half_i)
                nc.vector.tensor_tensor(h_pair(j), h_pair(j), u[:, :, :], ALU.add).then_inc(h_ready, 1)
                if more:
                    dve.wait_ge(sq_ready, j + 33)
                    sum_squares().then_inc(acc_ready, 1)
                    next_lo(q, half_i, 3)

            with dve.Fori(0, 3) as i:
                final_step(i + last, 0, i * 2)
                final_step(i + last, 1, i * 2 + 1)
            final_step(last + 3, 0, 6)
            final_step(last + 3, 1, 7, False)
            dve.wait_ge(rms_ready, 5)
            then(nc.vector.reciprocal(rstd[:, :], rms[:, :]))
            dve.wait_ge(hg_ready, PAIRS)
            for j in range(PAIRS):
                nc.vector.tensor_tensor(h_pair(j), h_pair(j), bc2(rstd[:, :]), ALU.mult).then_inc(final_ready, 1)

        @block.tensor
        def _(pe):
            def products(q, half_i, s, operand, ready_sem, ready, late=False):
                pe.wait_ge(lo_ready, (q * 2 + half_i) * CHUNKS + s + 1)
                if s == 0 and not (isinstance(q, int) and q == 0):
                    pe.wait_ge(psum_free, q * 2 + half_i - 1)
                pe.wait_ge(ready_sem, ready + 2 * s + 2)
                hi, lo = late_w if late else (w_hi[:, s], w_lo[:, s])
                for b in range(2):
                    bank = ps[:, 2 * half_i + b, :]
                    for k in range(CH_KT):
                        kt = s * CH_KT + k
                        cols = slice(b * PART, b * PART + PART)
                        nc.tensor.matmul(bank[:, :], hi[:, k, cols], operand[:, :, kt, :],
                                         start=kt == 0, stop=False)
                        last = nc.tensor.matmul(bank[:, TOK:2 * TOK], lo[:, k, cols], operand[:, 0, kt, :],
                                                start=False, stop=kt == KT - 1)
                last.then_inc(wts_used, 1)

            def pair(q, half_i, operand, ready_sem, ready, between=None):
                for s in range(CHUNKS):
                    products(q, half_i, s, operand, ready_sem, ready)
                    if between and s in between:
                        between[s]()

            def quad(q, operand, ready_sem, ready, between=None):
                pair(q, 0, operand, ready_sem, ready, between)
                pair(q, 1, operand, ready_sem, ready)

            def three(out, hi_w, lo_w, hi_x, lo_x, first, last):
                nc.tensor.matmul(out, hi_w, hi_x, start=first, stop=False)
                nc.tensor.matmul(out, hi_w, lo_x, start=False, stop=False)
                return nc.tensor.matmul(out, lo_w, hi_x, start=False, stop=last)

            def stats(n):
                pe.wait_ge(acc_ready, 8 * (n + 1))
                nc.tensor.matmul(x3[:, 0:TOK], ones[:, :], acc[:, 0, :], start=True, stop=False)
                nc.tensor.matmul(x3[:, 0:TOK], ones[:, :], acc[:, 1, :], start=False, stop=True
                                 ).then_inc(stats_done, 1)

            def rotate(n):
                pe.wait_ge(rope_in, n + 1)
                nc.tensor.matmul(x3, swap, u[:, :, :], start=True, stop=True).then_inc(rotated, 1)

            def transpose_v():
                pe.wait_ge(vt_ready, 1)
                for b in range(2):
                    for c in range(4):
                        last = nc.tensor.transpose(xs[:, b, c * PART:(c + 1) * PART], vt[:, b, HD * c:HD * c + PART],
                                                   ident)
                last.then_inc(v_transposed, 1)

            def scores(j, g):
                pe.wait_ge(q_ready, j + 1)
                if isinstance(j, int) and j == 0:
                    pe.wait_ge(v_read, 1)
                    pe.wait_ge(k_ready, 1)
                else:
                    pe.wait_ge(pt_ready, j)
                for b in range(2):
                    for t in range(2):
                        for e in range(2):
                            q_hi_t = qz[:, 0, 2 * b + t, HD * e:HD * e + PART]
                            q_lo_t = qz[:, 1, 2 * b + t, HD * e:HD * e + PART]
                            band = slice(HD * (2 * t + e), HD * (2 * t + e) + PART)
                            k_h = kpad[:, 0, bass.ds(g, 1), :, band].rearrange("p o a k -> p (o a) k")
                            k_l = kpad[:, 1, bass.ds(g, 1), :, band].rearrange("p o a k -> p (o a) k")
                            last = three(xs[:, b, t * TOK:(t + 1) * TOK], q_hi_t, q_lo_t, k_h, k_l, e == 0, e == 1)
                last.then_inc(scored, 1)

            def transpose_probs(j):
                pe.wait_ge(probs_ready, j + 1)
                for b in range(2):
                    for t in range(2):
                        for a in range(2):
                            m = 4 * b + 2 * t + a
                            at = a * TOK + t * PART
                            last = nc.tensor.transpose(xs[:, b, at:at + PART], prob[:, m * PART:(m + 1) * PART], ident)
                last.then_inc(transposed, 1)

            def attend(j, g):
                pe.wait_ge(pt_ready, j + 1)
                pe.wait_ge(vcur_ready, g + 1)
                if not (isinstance(j, int) and j == 0):
                    pe.wait_ge(mid_ready, j)
                for c in range(4):
                    out = x0.rearrange("p (b t) -> p b t", b=2)[:, :, c * HD:(c + 1) * HD]
                    for a in range(2):
                        v_cols = slice(HD, 3 * HD) if a == 0 else slice(0, 2 * HD)
                        p_cols = slice(a * TOK + c * HD, a * TOK + (c + 1) * HD)
                        last = three(out, vcur[:, 0, c, v_cols], vcur[:, 1, c, v_cols],
                                     pt[:, 0, :, p_cols], pt[:, 1, :, p_cols], a == 0, a == 1)
                last.then_inc(att_done, 1)

            qkv = (xn, xn_ready, 0)
            pe.wait_ge(consts_set, 2)
            with pe.Fori(0, WARM_UP):
                nc.tensor.matmul(x0[:, 0:PART], ones[:, :], ones[:, :], start=True, stop=True)
            pair(0, 0, *qkv)
            pair(0, 1, *qkv, {2: lambda: stats(0)})
            pe.wait_ge(const_loaded, 16)
            pair(1, 0, *qkv, {0: lambda: rotate(0), 2: transpose_v})

            def rotate_and_transpose(j, with_before):
                rotate(j + 1)
                if with_before:
                    transpose_probs(j - 1)

            def scores_and_output(j, g, g_before):
                scores(j, g)
                if g_before is not None:
                    attend(j - 1, g_before)

            def attention_pair(q, half_i, j, g, g_before):
                pair(q, half_i, *qkv, {1: lambda: rotate_and_transpose(j, g_before is not None),
                                       2: lambda: scores_and_output(j, g, g_before)})

            attention_pair(1, 1, 0, 0, None)
            with pe.Fori(2, Q_QKV) as q:
                attention_pair(q, 0, q * 2 - 3, q - 2, q - 2)
                attention_pair(q, 1, q * 2 - 2, q - 1, q - 2)

            def late_quad(q, operand, between):
                for half_i, s in ((0, 0), (0, 1), (0, 2), (1, 0), (1, 1), (1, 2), (0, 3), (1, 3)):
                    products(q, half_i, s, *operand, late=(half_i, s) == (1, 3))
                    if (half_i, s) in between:
                        between[half_i, s]()

            last_j, last_g = PAIRS - 1, KV_HEADS - 1
            att = (mid, mid_ready, MID_ATT)
            late_quad(QB_WO, att, {(0, 0): lambda: rotate(last_j + 1),
                                   (0, 1): lambda: transpose_probs(last_j - 1),
                                   (0, 2): lambda: scores_and_output(last_j, last_g, last_g),
                                   (1, 1): lambda: transpose_probs(last_j),
                                   (1, 2): lambda: attend(last_j, last_g)})
            with pe.Fori(1, Q_WO) as i:
                quad(i + QB_WO, *att)

            def mlp(base, norm, mid_base):
                operand = (xn, xn_ready, 8 * norm)
                quad(base, *operand, {3: lambda: stats(norm)})
                with pe.Fori(1, 4) as i:
                    quad(i + base, *operand)
                with pe.Fori(0, 4) as i:
                    quad(i + (base + 4), mid, mid_ready, mid_base)
                with pe.Fori(1, GROUPS) as g:
                    with pe.Fori(0, 4) as i:
                        quad(g * 8 + i + base, *operand)
                    with pe.Fori(0, 4) as i:
                        quad(g * 8 + i + (base + 4), mid, mid_ready, g * PAIRS + mid_base)

            mlp(QB_MLP0, 1, MID_MLP0)

            def gates(n):
                pe.wait_ge(gate_ready, n + 1)
                pe.wait_ge(xc_lo, n + 1)
                if not (isinstance(n, int) and n == 0):
                    pe.wait_ge(sig_done, n)
                for gate in range(2):
                    for b in range(2):
                        for k in range(2):
                            cols = slice(b * PART, b * PART + PART)
                            last = three(aux[:, gate, b * TOK:(b + 1) * TOK], gate_hi[:, 2 * gate + k, cols],
                                         gate_lo[:, 2 * gate + k, cols], xc_split[:, 0, k, :], xc_split[:, 1, k, :],
                                         k == 0, k == 1)
                last.then_inc(gates_done, 1)

            lru_in = (xn, xn_ready, 16)
            quad(QB_IN, *lru_in, {3: lambda: stats(2)})
            with pe.Fori(1, GATE_BLOCKS) as n:
                quad(n + QB_IN, *lru_in, {0: lambda: gates(n - 1)})
            lru_done = (mid, mid_ready, MID_LRU)
            late_quad(QB_OUT, lru_done, {(0, 0): lambda: gates(GATE_BLOCKS - 1)})
            with pe.Fori(1, Q_WO) as i:
                quad(i + QB_OUT, *lru_done)
            mlp(QB_MLP1, 3, MID_MLP1)
            pe.wait_ge(acc_ready, 5 * PAIRS - 1)
            for b in range(2):
                nc.tensor.matmul(x3[:, 0:TOK], ones[:, :], acc[:, b, :], start=b == 0, stop=False)
            pe.wait_ge(sq_ready, 5 * PAIRS)
            for b in range(2):
                last = nc.tensor.matmul(x3[:, 0:TOK], ones[:, :], sq[:, b, :], start=False, stop=b == 1)
            last.then_inc(stats_done, 1)


def _rope_tables():
    half = HD // 2
    freqs = (np.float32(10000.0) ** (-np.arange(half, dtype=np.float32) / np.float32(half))).astype(np.float32)
    ang = np.arange(TOK, dtype=np.float32)[:, None] * freqs[None, :]
    p = np.arange(PART)
    cos = np.cos(ang).astype(np.float32).T[p % half]
    sin = np.sin(ang).astype(np.float32).T[p % half] * np.where(p % HD < half, -1.0, 1.0)[:, None]
    swap = np.zeros((PART, PART), np.float32)
    swap[p, p ^ half] = 1.0
    return np.concatenate([cos, sin, swap, np.eye(PART)], axis=1).astype(np.float32)


def _columns(a):
    return np.asarray(a).reshape(-1, PART).T


def kernel(**inputs):
    import concourse.bacc as bacc
    from concourse.bass_utils import run_bass_kernel_spmd

    a = {k: np.asarray(v) for k, v in inputs.items()}
    x_l = np.ascontiguousarray(a["x"][0].T.reshape(KT, PART, TOK).transpose(1, 0, 2))
    sinks = np.broadcast_to(a["a_sinks"][0].reshape(PAIRS, 2, 1, 2), (PAIRS, 2, 2, 2)).reshape(1, 64)
    parts = [a["mix_norm"][0], a["mlp_norm"][0], a["mix_norm"][1], a["mlp_norm"][1], a["final_norm"],
             a["a_b_qkv"][0], a["a_b_o"][0], a["b_b_in"][0], a["b_conv_w"][0].reshape(-1), a["b_conv_b"][0],
             a["b_gate_a_b"][0], a["b_gate_x_b"][0], a["b_lambda"][0], a["b_b_out"][0]]
    vec = np.ascontiguousarray(np.concatenate([_columns(p) for p in parts]
                                              + [np.broadcast_to(sinks, (PART, 64))], axis=1))
    arrays = {"x_l": x_l, "vec": vec, "const": _rope_tables()}
    for name in ("a_w_qkv", "a_w_o", "b_w_in", "b_gate_a_w", "b_gate_x_w", "b_w_out", "mlp_w_up", "mlp_w_down"):
        arrays[name] = np.ascontiguousarray(a[name])
    nc = bacc.Bacc("TRN2", target_bir_lowering=False, num_devices=1)
    arrays = {f"{n}_dram": v for n, v in arrays.items()}
    args = [nc.dram_tensor(n, v.shape, mybir.dt.from_np(v.dtype), kind="ExternalInput").ap()
            for n, v in arrays.items()]
    out = nc.dram_tensor("out_l", (PART, KT, TOK), F32, kind="ExternalOutput").ap()
    build(nc, *args, out)
    r = run_bass_kernel_spmd(nc, [arrays], core_ids=[0])
    y = r.results[0]["out_l"]
    return np.ascontiguousarray(y.transpose(1, 0, 2).reshape(D, TOK).T).reshape(1, TOK, D)
```
